# Optimizing a Trainium2 kernel written in Bass

```python
import math
import jax, jax.numpy as jnp
from jax import lax
import numpy as np

D_MODEL = 1024
BATCH = 1
SEQ = 256
DEPTH = 1

MOBA_HEADS = 8
MOBA_HEAD_DIM = 64
MOBA_WIDTH = MOBA_HEADS * MOBA_HEAD_DIM
MOBA_BLOCK = 256
MOBA_TOPK = 3
MOBA_QCHUNK = 16
HGRN_HEADS = 4
HGRN_EXPAND = 128
HGRN_HEAD_DIM = 128
HGRN_WIDTH = HGRN_HEADS * HGRN_EXPAND
HGRN_CHUNK = 64
IN_SIZES = (MOBA_WIDTH, MOBA_WIDTH, MOBA_WIDTH,
            HGRN_WIDTH, HGRN_WIDTH, HGRN_WIDTH, HGRN_WIDTH,
            D_MODEL, D_MODEL)
IN_COLS = sum(IN_SIZES)
PEER_HEADS = 8
PEER_NKEYS = 128
PEER_EXPERTS = PEER_NKEYS * PEER_NKEYS
PEER_KEY_DIM = 128
PEER_HALF = PEER_KEY_DIM // 2
PEER_TOPK = 16
PEER_TOKEN_CHUNK = 512
DEEPNORM_ALPHA = (2.0 * DEPTH) ** 0.25
DEEPNORM_BETA = (8.0 * DEPTH) ** -0.25
LN_EPS = 1e-5
RMS_EPS = 1e-6

kernel_name = "hybrid_moba_hgrn2_peer_deepnorm_adaln"

F32 = jnp.float32

def layer_norm(x, g, b):
    xf = x.astype(F32)
    mu = jnp.mean(xf, -1, keepdims=True)
    var = jnp.mean(jnp.square(xf - mu), -1, keepdims=True)
    y = (xf - mu) * lax.rsqrt(var + LN_EPS)
    return (y * g.astype(F32) + b.astype(F32)).astype(x.dtype)

def alibi_slopes(n_heads):
    return jnp.exp2(-8.0 * jnp.arange(1, n_heads + 1, dtype=F32) / n_heads)

def moba_attention(q, k, v):
    B, S, H, dh = q.shape
    BS = MOBA_BLOCK
    nb = -(-S // BS)
    s_pad = nb * BS
    pad = ((0, 0), (0, s_pad - S), (0, 0), (0, 0))
    q = jnp.pad(q, pad).transpose(0, 2, 1, 3) * (dh ** -0.5)
    k = jnp.pad(k, pad).transpose(0, 2, 1, 3)
    v = jnp.pad(v, pad).transpose(0, 2, 1, 3)
    kb = k.reshape(B, H, nb, BS, dh)
    vb = v.reshape(B, H, nb, BS, dh)
    kmean = jnp.mean(kb.astype(F32), axis=3)
    gate = jnp.einsum('bhsd,bhnd->bhsn', q.astype(F32), kmean)
    qblk = jnp.arange(s_pad) // BS
    past = jnp.arange(nb)[None, :] < qblk[:, None]
    gate = jnp.where(past, gate, -jnp.inf)
    topk = min(MOBA_TOPK, nb)
    gval, gidx = lax.top_k(gate, topk)
    gvalid = jnp.isfinite(gval)
    slopes = alibi_slopes(H)
    bi = jnp.arange(B)[:, None, None, None]
    hi = jnp.arange(H)[None, :, None, None]
    offs = jnp.arange(BS)
    QC = MOBA_QCHUNK
    n_q = s_pad // QC

    def chunk(ci):
        p = ci * QC
        qc = lax.dynamic_slice_in_dim(q, p, QC, axis=2)
        idx = lax.dynamic_slice_in_dim(gidx, p, QC, axis=2)
        val = lax.dynamic_slice_in_dim(gvalid, p, QC, axis=2)
        qpos = p + jnp.arange(QC)
        j = p // BS
        k_own = lax.dynamic_index_in_dim(kb, j, axis=2, keepdims=False)
        v_own = lax.dynamic_index_in_dim(vb, j, axis=2, keepdims=False)
        dist_own = (qpos[:, None] - (j * BS + offs)[None, :]).astype(F32)
        s_own = (jnp.einsum('bhqd,bhkd->bhqk', qc, k_own).astype(F32)
                 - slopes[None, :, None, None] * dist_own[None, None])
        s_own = jnp.where(dist_own[None, None] >= 0, s_own, -jnp.inf)
        k_sel = kb[bi, hi, idx]
        v_sel = vb[bi, hi, idx]
        kpos_sel = idx[..., None] * BS + offs
        dist_sel = (qpos[None, None, :, None, None] - kpos_sel).astype(F32)
        s_sel = (jnp.einsum('bhqd,bhqnkd->bhqnk', qc, k_sel).astype(F32)
                 - slopes[None, :, None, None, None] * dist_sel)
        s_sel = jnp.where(val[..., None], s_sel, -jnp.inf)
        scores = jnp.concatenate([s_own, s_sel.reshape(B, H, QC, topk * BS)], axis=-1)
        probs = jax.nn.softmax(scores, axis=-1).astype(v.dtype)
        p_own = probs[..., :BS]
        p_sel = probs[..., BS:].reshape(B, H, QC, topk, BS)
        return (jnp.einsum('bhqk,bhkd->bhqd', p_own, v_own)
                + jnp.einsum('bhqnk,bhqnkd->bhqd', p_sel, v_sel))

    out = lax.map(chunk, jnp.arange(n_q))
    out = out.transpose(1, 0, 3, 2, 4).reshape(B, s_pad, H, dh)[:, :S]
    return out.reshape(B, S, H * dh)

def hgrn2(q, f_logit, i, g, lb, norm_g):
    B, S, _ = q.shape
    H, dk, dv, C = HGRN_HEADS, HGRN_EXPAND, HGRN_HEAD_DIM, HGRN_CHUNK
    nC = S // C

    def heads(t, d):
        return t.astype(F32).reshape(B, nC, C, H, d).transpose(0, 3, 1, 2, 4)

    lbf = lb.astype(F32)
    f = lbf + (1.0 - lbf) * jax.nn.sigmoid(f_logit.astype(F32))
    qh = heads(jax.nn.silu(q.astype(F32)), dk)
    kh = heads(1.0 - f, dk)
    lfh = heads(jnp.log(f), dk)
    vh = heads(i, dv)
    b = jnp.cumsum(lfh, axis=3)
    b_last = b[:, :, :, -1:, :]
    b_ref = b[:, :, :, C // 2:C // 2 + 1, :]
    a = jnp.einsum('bhntd,bhnsd->bhnts', qh * jnp.exp(b - b_ref), kh * jnp.exp(b_ref - b))
    causal = jnp.tril(jnp.ones((C, C), dtype=bool))
    a = jnp.where(causal, a, 0.0)
    o_intra = jnp.einsum('bhnts,bhnsv->bhntv', a, vh)
    ds = jnp.einsum('bhnsd,bhnsv->nbhdv', kh * jnp.exp(b_last - b), vh)
    decay = jnp.exp(b_last[:, :, :, 0, :]).transpose(2, 0, 1, 3)

    def step(state, inp):
        d, dsc = inp
        return d[..., None] * state + dsc, state

    s0 = jnp.zeros((B, H, dk, dv), F32)
    _, s_prev = lax.scan(step, s0, (decay, ds))
    o_inter = jnp.einsum('bhntd,nbhdv->bhntv', qh * jnp.exp(b), s_prev)
    o = (o_intra + o_inter).transpose(0, 2, 3, 1, 4).reshape(B, S, H, dv)
    o = o * lax.rsqrt(jnp.mean(o * o, axis=-1, keepdims=True) + RMS_EPS)
    o = o.reshape(B, S, H * dv) * norm_g.astype(F32) * jax.nn.silu(g.astype(F32))
    return o.astype(q.dtype)

def peer(h, wq, subkeys, u_tab, v_tab):
    B, S, D = h.shape
    T = B * S
    tc = math.gcd(T, PEER_TOKEN_CHUNK)
    H, K, NK = PEER_HEADS, PEER_TOPK, PEER_NKEYS
    hf = h.reshape(T // tc, tc, D)

    def chunk(xc):
        q = (xc @ wq).astype(F32).reshape(tc, H, 2, PEER_HALF)
        s = jnp.einsum('thpd,hpnd->thpn', q, subkeys.astype(F32))
        sv, si = lax.top_k(s, K)
        cand = (sv[:, :, 0, :, None] + sv[:, :, 1, None, :]).reshape(tc, H, K * K)
        cidx = (si[:, :, 0, :, None] * NK + si[:, :, 1, None, :]).reshape(tc, H, K * K)
        best, pos = lax.top_k(cand, K)
        eidx = jnp.take_along_axis(cidx, pos, axis=-1)
        gates = jax.nn.softmax(best, axis=-1)
        u = u_tab[eidx]
        act = jax.nn.gelu(jnp.einsum('td,thkd->thk', xc, u).astype(F32), approximate=False)
        w = (gates * act).astype(xc.dtype)
        return jnp.einsum('thk,thkd->td', w, v_tab[eidx])

    return lax.map(chunk, hf).reshape(B, S, D)

def setup_inputs(seed: int = 0) -> dict:
    key = jax.random.key(seed)
    ks = jax.random.split(key, 20)
    D, L = D_MODEL, DEPTH
    n = jax.random.normal
    return {
        'x': n(ks[0], (BATCH, SEQ, D), F32),
        'c': n(ks[1], (BATCH, D), F32),
        'w_ada': n(ks[2], (L, D, 6 * D), F32) * (0.5 * D ** -0.5),
        'b_ada': n(ks[3], (L, 6 * D), F32) * 0.01,
        'w_in': n(ks[4], (L, D, IN_COLS), F32) * D ** -0.5,
        'w_branch_a': n(ks[5], (L, MOBA_WIDTH, D), F32) * (MOBA_WIDTH ** -0.5 * DEEPNORM_BETA),
        'w_branch_b': n(ks[6], (L, HGRN_WIDTH, D), F32) * (HGRN_WIDTH ** -0.5 * DEEPNORM_BETA),
        'w_out': n(ks[7], (L, D, D), F32) * (D ** -0.5 * DEEPNORM_BETA),
        'hgrn_lb': 1.0 + 0.1 * n(ks[8], (L + 1, HGRN_WIDTH), F32),
        'hgrn_norm_g': 1.0 + 0.01 * n(ks[9], (L, HGRN_WIDTH), F32),
        'ln1_g': 1.0 + 0.01 * n(ks[10], (L, D), F32),
        'ln1_b': 0.01 * n(ks[11], (L, D), F32),
        'peer_wq': n(ks[12], (L, D, PEER_HEADS * PEER_KEY_DIM), F32) * D ** -0.5,
        'peer_subkeys': n(ks[13], (L, PEER_HEADS, 2, PEER_NKEYS, PEER_HALF), F32) * PEER_HALF ** -0.5,
        'peer_u': n(ks[14], (L, PEER_EXPERTS, D), F32) * D ** -0.5,
        'peer_v': n(ks[15], (L, PEER_EXPERTS, D), F32) * DEEPNORM_BETA,
        'ln2_g': 1.0 + 0.01 * n(ks[16], (L, D), F32),
        'ln2_b': 0.01 * n(ks[17], (L, D), F32),
    }

def reference(x, c, w_ada, b_ada, w_in, w_branch_a, w_branch_b, w_out, hgrn_lb, hgrn_norm_g,
              ln1_g, ln1_b, peer_wq, peer_subkeys, peer_u, peer_v, ln2_g, ln2_b):
    B, S, D = x.shape
    lb_all = jnp.cumsum(jax.nn.softmax(hgrn_lb.astype(F32), axis=0), axis=0)
    split_at = [int(v) for v in np.cumsum(IN_SIZES)[:-1]]
    for l in range(DEPTH):
        ada = jax.nn.silu(c) @ w_ada[l] + b_ada[l]
        sh1, sc1, gt1, sh2, sc2, gt2 = jnp.split(ada[:, None, :], 6, axis=-1)
        h = x * (1.0 + sc1) + sh1
        proj = h @ w_in[l]
        qa, ka, va, hq, hf, hi, hg, ga, gb = jnp.split(proj, split_at, axis=-1)
        mh = (B, S, MOBA_HEADS, MOBA_HEAD_DIM)
        ya = moba_attention(qa.reshape(mh), ka.reshape(mh), va.reshape(mh))
        yb = hgrn2(hq, hf, hi, hg, lb_all[l], hgrn_norm_g[l])
        mixed = (jax.nn.sigmoid(ga) * (ya @ w_branch_a[l])
                 + jax.nn.sigmoid(gb) * (yb @ w_branch_b[l]))
        x = layer_norm(DEEPNORM_ALPHA * x + gt1 * (mixed @ w_out[l]), ln1_g[l], ln1_b[l])
        h2 = x * (1.0 + sc2) + sh2
        y = peer(h2, peer_wq[l], peer_subkeys[l], peer_u[l], peer_v[l])
        x = layer_norm(DEEPNORM_ALPHA * x + gt2 * y, ln2_g[l], ln2_b[l])
    return x


_drawn_inputs = setup_inputs


def setup_inputs(seed=0):
    import zlib

    import numpy as np

    out = dict(_drawn_inputs(seed))
    spreads = {}
    factors = {'b_ada': 5.304,
     'hgrn_lb': 23.841,
     'hgrn_norm_g': 200.0,
     'ln1_g': 66.909,
     'ln1_b': 66.349,
     'ln2_g': 194.414,
     'ln2_b': 188.271,
     'w_branch_a': 2.78}
    for name, (base, spread) in spreads.items():
        noise = np.random.default_rng([zlib.crc32(name.encode()), seed]).standard_normal(out[name].shape)
        drawn = base * np.exp(spread * noise) if base else spread * noise
        out[name] = __import__('jax').numpy.asarray(drawn.astype(out[name].dtype))
    for name, factor in factors.items():
        out[name] = (out[name] * factor).astype(out[name].dtype)
    return out
```

```python
from contextlib import ExitStack

import concourse.bass as bass
from concourse import mybir

P = 128
F32 = mybir.dt.float32
F32R = mybir.dt.float32r
U32 = mybir.dt.uint32
I32 = mybir.dt.int32
ALU = mybir.AluOpType
ACT = mybir.ActivationFunctionType
AX = mybir.AxisListType.X

T = 256
TT = T // P
D = 1024
KC = D // P
HEADS = 8
DH = 64
HG = 4
CH = 64
NCH = T // CH
NK = 128
PH = 8
TOPK = 16
ALPHA = 2.0 ** 0.25
LN_EPS = 1e-5
RMS_EPS = 1e-6
NEG = -3.0e38
FAR = 1.0e30

HF, HQ, HI, HGATE, QA, KA, VA, GA, GB = 0, 2, 4, 6, 8, 10, 12, 14, 18
BRANCH, WOUT, WQ, NA = 22, 26, 30, 34
NATURAL = set(range(HI, HI + 2)) | set(range(HGATE, HGATE + 2)) | set(range(VA, VA + 2)) | set(range(WOUT, WQ))
DVE_EVAC = set(range(HQ, HQ + 2)) | set(range(HGATE, HGATE + 2)) | set(range(BRANCH, WQ))
NG = NK // 2
G1 = NG // 2
U0 = NA
U2 = U0 + G1 + 1
STEPS = NG - 1 - G1
V2 = U2 + 2 * STEPS
S_RAW, S_PIECE = 2, 4
GROUPS = T // 4

ADA_W, ADA_SLOTS = 1024, 4
ADA_TILES = 6 * D // ADA_W * KC
ADA_THIRD = ADA_TILES // 3


def ada_tile(t):
    third, r = divmod(t, ADA_THIRD)
    k, half = divmod(r, 2)
    return third, k, half


def evac_count(b):
    mine = b in DVE_EVAC
    return sum(1 for x in range(b + 1) if (x in DVE_EVAC) == mine)


def ada_at(b):
    first = ADA_THIRD
    out = []
    for x in range(2, 22):
        n = 2 if x < 14 else 1
        if x == b:
            out = list(range(first, first + n))
        first += n
    assert first == ADA_TILES
    return out


def layer(nc, xT_d, x_d, c_d, w_ada_d, b_ada_d, ws_d, lb_d, norm_g_d, ln1_g_d, ln1_b_d,
          keys_d, u_d, v_d, ln2_g_d, ln2_b_d, x1_d, gt2_d, out_d):
    with ExitStack() as ctx:
        base = nc.sbuf_base + (-nc.sbuf_base) % 64

        def sb(name, at, shape, dt=F32):
            return nc.alloc_sbuf_tensor_at(name, [P] + list(shape), dt, offset=base + 4 * at)

        def sem(name):
            return ctx.enter_context(nc.semaphore(name))

        raw = sb("raw", 0, [S_RAW, 2, 1024])
        w_hi = sb("w_hi", 4096, [S_PIECE, 1024], F32R)
        w_lo = sb("w_lo", 8192, [S_PIECE, 1024], F32R)
        a_hi = sb("a_hi", 12288, [KC, T], F32R)
        a_lo = sb("a_lo", 14336, [KC, T], F32R)
        SM, AR = 16384, 17408
        small_at = [SM]

        def small(name, n, dt=F32):
            at = small_at[0]
            small_at[0] += -(-n // 8) * 8
            assert small_at[0] <= AR
            return sb(name, at, [n], dt)

        ident = small("ident", P)
        iota = small("iota", P)
        c_col = small("c_col", KC)
        c_sig = small("c_sig", KC)
        sc_col = small("sc_col", KC)
        ones_col = small("ones_col", 1)
        ones_pp = small("ones_pp", P)
        j_col = small("j_col", 4)
        lb_raw = small("lb_raw", 2 * HG)
        lb_max = small("lb_max", HG)
        lb_e = small("lb_e", 2 * HG)
        lb_col = small("lb_col", HG)
        om_lb = small("om_lb", HG)
        mod1 = small("mod1", 2 * KC)
        mod2 = small("mod2", 2 * KC)
        decay = small("decay", HG * NCH)
        rmax = small("rmax", 2 * TT)
        rsum = small("rsum", 2 * TT)
        rinv = small("rinv", 2 * TT)
        sumsq = small("sumsq", TT * HG)
        rms = small("rms", TT * HG)
        rms_i = small("rms_i", TT * HG)
        bn = small("bn", TT * 2 * 6)
        mv = small("mv", TT * 2)
        std = small("std", TT)
        rstd = small("rstd", TT)
        gsum = small("gsum", TT * PH)
        ginv = small("ginv", TT * PH)
        lf = sb("lf", AR + 0, [HG * T])
        o_nat = sb("o_nat", AR + 0, [TT, HG * P])
        bcum = sb("bcum", AR + 1024, [HG * T])
        kl_nat = sb("kl_nat", AR + 1024, [TT, HG, P])
        qh = sb("qh", AR + 2048, [HG * T])
        kh = sb("kh", AR + 3072, [HG * T])
        q_e = sb("q_e", AR + 4096, [HG * T])
        k_e = sb("k_e", AR + 5120, [HG * T])
        k_l = sb("k_l", AR + 6144, [HG * T])
        q_x = sb("q_x", AR + 7168, [HG * T])
        vh = sb("vh", AR + 8192, [TT, HG * P])
        sgh = sb("sgh", AR + 9216, [TT, HG * P])
        aT = sb("aT", AR + 10240, [TT, HG, P])
        state = sb("state", AR + 11264, [NCH - 1, HG * P])
        qT = sb("qT", AR + 12800, [HG, T])
        kT = sb("kT", AR + 13824, [HG, T])
        va = sb("va", AR + 14848, [TT, HEADS * DH])
        prob = sb("prob", AR + 15872, [2, 3 * P])
        pT = sb("pT", AR + 16640, [3 * P])
        dist = sb("dist", AR + 17024, [3 * P])
        xT = sb("xT", AR + 17408, [KC, T])
        sig_a = sb("sig_a", AR + 17408, [KC, T])
        sig_b = sb("sig_b", AR + 19456, [KC, T])
        ada = sb("ada", AR + 21504, [ADA_SLOTS, ADA_W])
        acc = sb("acc", AR + 25600, [2, 2 * ADA_W])
        x_nat = sb("x_nat", AR + 21504, [TT, D])
        ln1_g = sb("ln1_g", AR + 23552, [D])
        ln1_b = sb("ln1_b", AR + 24576, [D])
        norm_g = sb("norm_g", AR + 29696, [HG * P])
        scan_m = sb("scan_m", AR + 30208, [HG * T])
        m_hi = sb("m_hi", AR + 30208, [KC, T], F32R)
        m_lo = sb("m_lo", AR + 32256, [KC, T], F32R)
        yaT = sb("yaT", AR + 34304, [HG, T])
        gt1 = sb("gt1", AR + 4096, [D])
        gt2_row = sb("gt2_row", AR + 5120, [D])
        br_a = sb("br_a", AR + 6144, [2 * T])
        br_b = sb("br_b", AR + 6656, [2 * T])
        mix = sb("mix", AR + 7168, [2 * T])
        x1 = sb("x1", AR + 25600, [TT, D])
        h2f = sb("h2f", AR + 22528, [KC, T])
        score = sb("score", AR + 16384, [TT * PH, 2 * NK])
        qpT = sb("qpT", AR + 20480, [PH, T])
        keys = sb("keys", AR + 27648, [PH, 2 * NK])
        R0 = AR + 29696
        s_in = sb("s_in", R0, [2, NK])
        s_cut = sb("s_cut", R0 + 256, [2, NK])
        cand = sb("cand", R0 + 512, [TOPK, TOPK])
        c_cut = sb("c_cut", R0 + 768, [TOPK * TOPK])
        eq = sb("eq", R0 + 1024, [2, TOPK, TOPK])
        top_v = sb("top_v", R0 + 1536, [2, TOPK])
        top_i = sb("top_i", R0 + 1568, [2, TOPK], U32)
        top_f = sb("top_f", R0 + 1600, [2, TOPK])
        pos = sb("pos", R0 + 1632, [TOPK], U32)
        pos2 = sb("pos2", R0 + 1648, [2, TOPK], U32)
        posf = sb("posf", R0 + 1680, [2, TOPK])
        best = sb("best", R0 + 1712, [TT * PH, TOPK])
        gate = sb("gate", R0 + 1968, [TT * PH, TOPK])
        ij = sb("ij", R0 + 2224, [2, TT * PH, TOPK])
        best_t = sb("best_t", R0 + 2736, [TOPK])
        assert R0 + 2736 + TOPK <= AR + 32768
        W = sb("W", AR, [NK, T])
        ws_hi = sb("ws_hi", AR + 32768, [2, T], F32R)
        ws_lo = sb("ws_lo", AR + 33280, [2, T], F32R)
        oh_i = [sb("oh_i0", AR + 33792, [4, P]), sb("oh_i1", AR + 32768, [4, P])]
        oh_j = [sb("oh_j0", AR + 34304, [4, P]), sb("oh_j1", AR + 33280, [4, P])]
        idx = sb("idx", AR + 34816, [3, T])
        gel = sb("gel", AR + 33792, [2 * T])
        assert base + 4 * (AR + 34816 + 768) <= nc.sbuf_usable_end
        E0 = AR + NG * T
        x1_b = sb("x1_b", E0, [TT, D])
        gt2_b = sb("gt2_b", E0 + 2048, [D])
        ln2_g = sb("ln2_g", E0 + 3072, [D])
        ln2_b = sb("ln2_b", E0 + 4096, [D])
        z2 = sb("z2", E0 + 5120, [TT, D])

        def bank(name):
            return ctx.enter_context(nc.psum_tensor(name, [P, 512], F32))

        pw = [bank("pw0"), bank("pw1")]
        pv = [bank("pv0"), bank("pv1")]
        px = [bank("px0"), bank("px1"), bank("px2"), bank("px3")]

        raw_landed = [sem("raw_landed0"), sem("raw_landed1")]
        hi_ready, lo_ready = sem("hi_ready"), sem("lo_ready")
        piece_used = sem("piece_used")
        act_took, dve_took = sem("act_took"), sem("dve_took")
        small_landed, xT_landed, norm_landed = sem("small_landed"), sem("xT_landed"), sem("norm_landed")
        bias_landed = [sem(f"bias_landed{g}") for g in range(3)]
        ada_landed = [sem(f"ada_landed{s}") for s in range(ADA_SLOTS)]
        ada_done = sem("ada_done")
        acc_cleared = sem("acc_cleared")
        consts = sem("consts")
        pool_chain, dve_chain, act_chain = sem("pool_chain"), sem("dve_chain"), sem("act_chain")
        iota_f = sem("iota_f")
        lb_e_ready, c_sig_ready, lb_max_ready = sem("lb_e_ready"), sem("c_sig_ready"), sem("lb_max_ready")
        mod1_ready, h_ready = sem("mod1_ready"), sem("h_ready")
        act_hi, act_lo = sem("act_hi"), sem("act_lo")
        sig_done = sem("sig_done")
        f_ready, lf_ready, d_ready, e_ready, qk_ready = (sem(s) for s in (
            "f_ready", "lf_ready", "d_ready", "e_ready", "qk_ready"))
        aT_done, aT_copied, aT_ready = sem("aT_done"), sem("aT_copied"), sem("aT_ready")
        kl_done, kl_ready = sem("kl_done"), sem("kl_ready")
        ds_done, state_ready = sem("ds_done"), sem("state_ready")
        o_done, o_copied, ss_ready, rms_ready, yb_ready, ybT_done = (sem(s) for s in (
            "o_done", "o_copied", "ss_ready", "rms_ready", "yb_ready", "ybT_done"))
        s_done, s_max, p_exp, p_ready, pT_done, pT_ready, pv_done, ya_copied = (sem(s) for s in (
            "s_done", "s_max", "p_exp", "p_ready", "pT_done", "pT_ready", "pv_done", "ya_copied"))
        gt1_done, gt2_done, mod2_done, mod2_ready, gt1_ready, gt2_ready = (sem(s) for s in (
            "gt1_done", "gt2_done", "mod2_done", "mod2_ready", "gt1_ready", "gt2_ready"))
        gates_ready, mix_ready, m_hi_ready, m_lo_ready = (sem(s) for s in (
            "gates_ready", "mix_ready", "m_hi_ready", "m_lo_ready"))
        x_landed, keys_cleared, keys_landed = sem("x_landed"), sem("keys_cleared"), sem("keys_landed")
        var_ready, std_ready, x1_ready, x1T_done, h2f_ready = (sem(s) for s in (
            "var_ready", "std_ready", "x1_ready", "x1T_done", "h2f_ready"))
        gt2_spilled, x1_spilled = sem("gt2_spilled"), sem("x1_spilled")
        out_done = sem("out_done")
        score_done, score_copied = sem("score_done"), sem("score_copied")
        u_taken = sem("u_taken")
        s_in_ready, s_in_used = sem("s_in_ready"), sem("s_in_used")
        best_ready, gate_exp, gate_ready = sem("best_ready"), sem("gate_exp"), sem("gate_ready")
        idxT_done, idx_ready = sem("idxT_done"), sem("idx_ready")
        ohi_ready, ohj_ready, oh_used, g_lo_taken, g_hi_taken = (sem(s) for s in (
            "ohi_ready", "ohj_ready", "oh_used", "g_lo_taken", "g_hi_taken"))
        gel_ready, prod_ready = sem("gel_ready"), sem("prod_ready")
        wsplit_hi, wsplit_lo = sem("wsplit_hi"), sem("wsplit_lo")
        end_landed, y_done = sem("end_landed"), sem("y_done")
        var2_ready, std2_ready, z2_ready = sem("var2_ready"), sem("std2_ready"), sem("z2_ready")

        block = ctx.enter_context(nc.Block())

        def dest(n):
            return raw[:, n % S_RAW].rearrange("p h n -> p (h n)")

        def u_src(g):
            return u_d[bass.ds(g, 1)].rearrange("a p n -> p (a n)")

        def v_src(g):
            return v_d[bass.ds(g, 1)].rearrange("a p n -> p (a n)")

        @block.sync
        def _(sp):
            def raw_free(n):
                sp.wait_ge(hi_ready, 2 * n - 2)
                sp.wait_ge(lo_ready, 2 * n - 2)

            def load_block(n):
                if n >= S_RAW:
                    raw_free(n)
                sp.dma_start(dest(n), ws_d[n]).then_inc(raw_landed[n % S_RAW], 16)

            def load_ada(t):
                third, k, half = ada_tile(t)
                if t >= ADA_SLOTS:
                    sp.wait_ge(ada_done, t - ADA_SLOTS + 1)
                col = third * 2 * ADA_W + half * ADA_W
                sp.dma_start(ada[:, t % ADA_SLOTS], w_ada_d[k * P:(k + 1) * P, col:col + ADA_W]) \
                    .then_inc(ada_landed[t % ADA_SLOTS], 16)

            def load_bias(g):
                sp.wait_ge(acc_cleared, g + 1)
                sp.dma_start(acc[0:1, g % 2], b_ada_d[0:1, g * 2 * ADA_W:(g + 1) * 2 * ADA_W]) \
                    .then_inc(bias_landed[g], 16)

            sp.dma_start(c_col[:, :], c_d).then_inc(small_landed, 16)
            sp.dma_start(lb_raw[:, :], lb_d).then_inc(small_landed, 16)
            for t in range(4):
                load_ada(t)
            load_bias(0)
            for t in range(4, 12):
                load_ada(t)
            sp.dma_start(xT[:, :, :], xT_d.rearrange("(k p) t -> p k t", p=P)).then_inc(xT_landed, 16)
            for t in range(12, ADA_THIRD):
                load_ada(t)
            load_block(0)
            load_block(1)
            load_bias(1)
            sp.dma_start(norm_g[:, :], norm_g_d.partition_broadcast(P)).then_inc(norm_landed, 16)
            for b in range(2, NA):
                for t in ada_at(b):
                    if t == 2 * ADA_THIRD:
                        load_bias(2)
                    load_ada(t)
                load_block(b)
                if b == BRANCH:
                    sp.wait_ge(ada_done, ADA_TILES)
                    sp.dma_start(x_nat[:, :, :], x_d.rearrange("(a p) n -> p a n", p=P)).then_inc(x_landed, 16)
                    sp.dma_start(ln1_g[:, :], ln1_g_d.partition_broadcast(P)).then_inc(x_landed, 16)
                    sp.dma_start(ln1_b[:, :], ln1_b_d.partition_broadcast(P)).then_inc(x_landed, 16)
                if b == WOUT:
                    sp.wait_ge(keys_cleared, 1)
                    for half in range(2):
                        q = slice(half * DH, (half + 1) * DH)
                        sp.dma_start(keys[q, :, half * NK:(half + 1) * NK], keys_d[q]).then_inc(keys_landed, 16)
            with sp.Fori(0, G1 // 2) as i:
                for e in range(2):
                    raw_free(2 * i + (U0 + e))
                    sp.dma_start(dest(U0 + e), u_src(2 * i + e)).then_inc(raw_landed[(U0 + e) % S_RAW], 16)
            raw_free(U0 + G1)
            sp.dma_start(dest(U0 + G1), u_src(G1)).then_inc(raw_landed[(U0 + G1) % S_RAW], 16)
            with sp.Fori(0, STEPS) as q:
                raw_free(2 * q + U2)
                sp.dma_start(dest(U2), u_src(q + (G1 + 1))).then_inc(raw_landed[U2 % S_RAW], 16)
                raw_free(2 * q + (U2 + 1))
                sp.dma_start(dest(U2 + 1), v_src(q + G1)).then_inc(raw_landed[(U2 + 1) % S_RAW], 16)
            raw_free(V2)
            sp.dma_start(dest(V2), v_src(NG - 1)).then_inc(raw_landed[V2 % S_RAW], 16)
            with sp.Fori(0, G1 // 2) as i:
                for e in range(2):
                    raw_free(2 * i + (V2 + 1 + e))
                    sp.dma_start(dest(V2 + 1 + e), v_src(2 * i + e)).then_inc(raw_landed[(V2 + 1 + e) % S_RAW], 16)
            for t in range(TT):
                sp.wait_ge(z2_ready, t + 1)
                sp.dma_start(out_d[t * P:(t + 1) * P, :], z2[:, t]).then_inc(out_done, 16)
            sp.wait_ge(out_done, 16 * TT)

        @block.gpsimd
        def _(pool):
            n = [0]

            def link(ins):
                n[0] += 1
                ins.then_inc(pool_chain, 1)
                pool.wait_ge(pool_chain, n[0])

            for g in range(2):
                nc.gpsimd.memset(acc[:, g], 0.0).then_inc(acc_cleared, 1)
            nc.gpsimd.memset(ones_pp[:, :], 1.0)
            nc.gpsimd.memset(ones_col[:, :], 1.0).then_inc(consts, 1)
            link(nc.gpsimd.memset(ident[:, :], 0.0))
            nc.gpsimd.affine_select(out=ident[:, :], in_=ident[:, :], compare_op=ALU.not_equal, fill=1.0,
                                    base=0, pattern=[[-1, P]], channel_multiplier=1).then_inc(consts, 1)
            link(nc.gpsimd.iota(dist[:, 0:P].bitcast(I32), pattern=[[-1, P]], base=0, channel_multiplier=1))
            link(nc.gpsimd.iota(dist[:, P:3 * P].bitcast(I32), pattern=[[-1, 2 * P]], base=P, channel_multiplier=1))
            link(nc.gpsimd.tensor_copy(dist[:, :], dist[:, :].bitcast(I32)))
            link(nc.gpsimd.affine_select(out=dist[:, 0:P], in_=dist[:, 0:P], compare_op=ALU.is_ge, fill=FAR,
                                         base=0, pattern=[[-1, P]], channel_multiplier=1))
            nc.gpsimd.affine_select(out=dist[:, P:3 * P], in_=dist[:, P:3 * P], compare_op=ALU.is_ge, fill=FAR,
                                    base=P, pattern=[[-1, 2 * P]], channel_multiplier=1).then_inc(consts, 1)
            link(nc.gpsimd.iota(iota[:, :].bitcast(I32), pattern=[[1, P]], base=0, channel_multiplier=0))
            nc.gpsimd.tensor_copy(iota[:, :], iota[:, :].bitcast(I32)).then_inc(consts, 1)
            link(nc.gpsimd.memset(scan_m[:, :], 1.0))
            nc.gpsimd.memset(scan_m[:, :].rearrange("p (n c) -> p n c", c=CH)[:, :, 0:1], 0.0).then_inc(consts, 1)
            nc.gpsimd.memset(aT[:, :, :, :], 0.0).then_inc(consts, 1)
            pool.wait_ge(mod1_ready, 1)
            nc.gpsimd.memset(acc[:, 0], 0.0).then_inc(acc_cleared, 1)
            pool.wait_ge(aT_copied, TT)
            nc.gpsimd.affine_select(out=aT[:, :, :, :].rearrange("p a h t -> p (a h) t"),
                                    in_=aT[:, :, :, :].rearrange("p a h t -> p (a h) t"),
                                    compare_op=ALU.is_ge, fill=0.0, base=0,
                                    pattern=[[0, TT * HG], [1, P]], channel_multiplier=-1).then_inc(aT_ready, 1)
            pool.wait_ge(mod2_done, 1)
            pool.wait_ge(gt1_done, 1)
            nc.gpsimd.memset(keys[:, :, :], 0.0).then_inc(keys_cleared, 1)
            pool.wait_ge(gt2_ready, 1)
            pool.dma_start(gt2_d, gt2_row[0:1, :]).then_inc(gt2_spilled, 16)
            pool.wait_ge(x1_ready, TT)
            pool.dma_start(x1_d.rearrange("(a p) n -> p a n", p=P), x1[:, :, :]).then_inc(x1_spilled, 16)
            pool.wait_ge(gt2_spilled, 16)
            pool.wait_ge(x1_spilled, 16)
            pool.wait_ge(g_hi_taken, 2)
            start = n[0]
            with pool.Fori(0, GROUPS // 2) as i:
                for e in range(2):
                    pool.wait_ge(oh_used, 2 * i + (e + 1))
                    nc.gpsimd.tensor_copy(j_col[:, e:e + 1], idx[:, 1, bass.ds(8 * i + (4 * e + 3), 1)]).then_inc(pool_chain, 1)
                    pool.wait_ge(pool_chain, 2 * i + (start + e + 1))
                    nc.gpsimd.nop(nofuse=True)
                    nc.gpsimd.tensor_scalar(oh_j[e][:, 3], iota[:, :], j_col[:, e:e + 1], None, ALU.is_equal) \
                        .then_inc(ohj_ready, 1)
            pool.wait_ge(piece_used, 2 * V2 + 2)
            pool.dma_start(x1_b[:, :, :], x1_d.rearrange("(a p) n -> p a n", p=P)).then_inc(end_landed, 16)
            pool.dma_start(gt2_b[:, :], gt2_d.rearrange("a n -> (a n)").partition_broadcast(P)).then_inc(end_landed, 16)
            pool.dma_start(ln2_g[:, :], ln2_g_d.partition_broadcast(P)).then_inc(end_landed, 16)
            pool.dma_start(ln2_b[:, :], ln2_b_d.partition_broadcast(P)).then_inc(end_landed, 16)

        @block.scalar
        def _(act):
            def copy(out, in_, **kw):
                return nc.scalar.activation(out, in_, ACT.Copy, **kw)

            def split_hi(n, landed, slot_block):
                s = slot_block % S_RAW
                act.wait_ge(raw_landed[s], landed)
                for e in range(2):
                    m = 2 * n + e
                    if not isinstance(m, int) or m >= S_PIECE:
                        act.wait_ge(piece_used, m - S_PIECE + 1)
                    copy(w_hi[:, (2 * slot_block + e) % S_PIECE], raw[:, s, e]).then_inc(hi_ready, 1)

            act.wait_ge(lb_max_ready, 1)
            nc.scalar.activation(lb_e[:, :], lb_e[:, :], ACT.Exp).then_inc(lb_e_ready, 1)
            act.wait_ge(small_landed, 32)
            nc.scalar.activation(c_sig[:, :], c_col[:, :], ACT.Sigmoid).then_inc(c_sig_ready, 1)

            for b in range(NA):
                split_hi(b, 16 * (b // S_RAW + 1), b)
                if b == 1:
                    for half in range(2):
                        q = slice(half * KC // 2, (half + 1) * KC // 2)
                        act.wait_ge(h_ready, half + 1)
                        copy(a_hi[:, q], xT[:, q]).then_inc(act_hi, 1)
                e = b - 2
                if e >= 0:
                    s = e % 2
                    act.wait_ge(piece_used, 2 * e + 2)
                if HF <= e < HF + 2:
                    r = e - HF
                    nc.scalar.activation(lf[:, r * 512:(r + 1) * 512], pw[s][:, :], ACT.Sigmoid).then_inc(act_took, 1)
                if HQ <= e < HQ + 2:
                    r = e - HQ
                    nc.scalar.activation(qh[:, r * 512:(r + 1) * 512], pw[s][:, :], ACT.Sigmoid).then_inc(sig_done, 1)
                if HI <= e < HI + 2 or VA <= e < VA + 2:
                    dst, r = (vh, e - HI) if e < VA else (va, e - VA)
                    copy(dst[:, 0, r * 256:(r + 1) * 256], pw[s][:, 0:256])
                    copy(dst[:, 1, r * 256:(r + 1) * 256], pv[s][:, 0:256]).then_inc(act_took, 1)
                if HGATE <= e < HGATE + 2:
                    r = e - HGATE
                    for t, src in enumerate((pw[s], pv[s])):
                        last = nc.scalar.activation(sgh[:, t, r * 256:(r + 1) * 256], src[:, 0:256], ACT.Sigmoid)
                    last.then_inc(sig_done, 1)
                for lo, dst, scale in ((QA, qT, DH ** -0.5), (KA, kT, 1.0)):
                    if lo <= e < lo + 2:
                        r = e - lo
                        copy(dst[:, 2 * r:2 * r + 2], pw[s][:, :].rearrange("p (c t) -> p c t", c=2), scale=scale) \
                            .then_inc(act_took, 1)
                for lo, dst in ((GA, sig_a), (GB, sig_b)):
                    if lo <= e < lo + 4:
                        r = e - lo
                        copy(dst[:, 2 * r:2 * r + 2], pw[s][:, :].rearrange("p (c t) -> p c t", c=2)).then_inc(act_took, 1)
                if b == 10:
                    act.wait_ge(f_ready, 1)
                    nc.scalar.activation(lf[:, :], lf[:, :], ACT.Ln).then_inc(lf_ready, 1)
                if b == 11:
                    act.wait_ge(d_ready, 2)
                    nc.scalar.activation(k_e[:, :], q_e[:, :], ACT.Exp, scale=-1.0).then_inc(act_chain, 1)
                    act.wait_ge(act_chain, 1)
                    nc.scalar.activation(q_e[:, :], q_e[:, :], ACT.Exp)
                    nc.scalar.activation(k_l[:, :], k_l[:, :], ACT.Exp)
                    nc.scalar.activation(q_x[:, :], bcum[:, :], ACT.Exp)
                    nc.scalar.activation(decay[:, :], bcum[:, :].rearrange("p (n c) -> p n c", c=CH)[:, :, CH - 1],
                                         ACT.Exp).then_inc(e_ready, 1)
                if b == 16:
                    for t, src in enumerate((px[3], pv[0])):
                        act.wait_ge(aT_done, t + 1)
                        if t == 0:
                            act.wait_ge(consts, 6)
                        for c in range(2):
                            q = slice(c * CH, (c + 1) * CH)
                            last = copy(aT[q, t, :, c * CH:(c + 1) * CH],
                                        src[q, :].rearrange("p (h t) -> p h t", h=HG)[:, :, c * CH:(c + 1) * CH])
                        last.then_inc(aT_copied, 1)
                if b == 17:
                    for t, src in enumerate((pv[1], px[3])):
                        act.wait_ge(kl_done, t + 1)
                        copy(kl_nat[:, t], src[:, :].rearrange("p (h t) -> p h t", h=HG)).then_inc(kl_ready, 1)
                if b == 21:
                    for t, src in enumerate((px[3], pv[0])):
                        act.wait_ge(o_done, t + 1)
                        copy(o_nat[:, t], src[:, :]).then_inc(o_copied, 1)
                    act.wait_ge(ss_ready, 1)
                    nc.scalar.activation(rms[:, :], sumsq[:, :], ACT.Sqrt).then_inc(rms_ready, 1)
                h = b - 15
                if 0 <= h < HEADS:
                    act.wait_ge(s_max, h + 1)
                    x = h % 2
                    for t, q in enumerate((slice(0, P), slice(P, 3 * P))):
                        last = nc.scalar.activation(prob[:, x, q], prob[:, x, q], ACT.Exp,
                                                    bias=rmax[:, 2 * x + t:2 * x + t + 1],
                                                    accum_out=rsum[:, 2 * x + t:2 * x + t + 1])
                    last.then_inc(p_exp, 1)
                h = b - 16
                if 0 <= h < HEADS:
                    act.wait_ge(pT_done, h + 1)
                    if h >= 1:
                        act.wait_ge(pv_done, h)
                    copy(pT[:, :], px[1][:, 0:3 * P]).then_inc(pT_ready, 1)
                for h in range(1, HEADS, 2):
                    if b == min(h + 17, 23):
                        act.wait_ge(pv_done, h + 1)
                        copy(yaT[:, h // 2], px[2][:, 0:T]).then_inc(ya_copied, 1)
                if b == 23:
                    act.wait_ge(ya_copied, HEADS // 2)
                    copy(a_hi[:, 0:4], yaT[:, :, :]).then_inc(act_hi, 1)
                    for t, src in enumerate((pv[1], px[3])):
                        act.wait_ge(ybT_done, t + 1)
                        last = copy(a_hi[:, 4:8, t * P:(t + 1) * P], src[:, :].rearrange("p (h t) -> p h t", h=HG))
                    last.then_inc(act_hi, 1)
                    for dst in (sig_a, sig_b):
                        act.wait_ge(act_took, evac_count(GB + 3))
                        last = nc.scalar.activation(dst[:, :, :], dst[:, :, :], ACT.Sigmoid)
                    last.then_inc(gates_ready, 1)
                if BRANCH <= e < BRANCH + 4:
                    r = e - BRANCH
                    act.wait_ge(mix_ready, r + 1)
                    copy(m_hi[:, 2 * r:2 * r + 2], mix[:, :].rearrange("p (c t) -> p c t", c=2)).then_inc(m_hi_ready, 1)
                if e == WOUT + 3:
                    act.wait_ge(var_ready, 1)
                    nc.scalar.activation(std[:, :], std[:, :], ACT.Sqrt).then_inc(std_ready, 1)
                    for half in range(2):
                        q = slice(half * KC // 2, (half + 1) * KC // 2)
                        act.wait_ge(h2f_ready, half + 1)
                        copy(a_hi[:, q], h2f[:, q]).then_inc(act_hi, 1)
                if WQ <= e:
                    r = e - WQ
                    copy(qpT[:, 2 * r:2 * r + 2], pw[s][:, :].rearrange("p (c t) -> p c t", c=2)).then_inc(act_took, 1)

            split_hi(U0, 16 * (U0 // S_RAW + 1), U0)
            for e in range(NA - 2, NA):
                act.wait_ge(piece_used, 2 * e + 2)
                r = e - WQ
                copy(qpT[:, 2 * r:2 * r + 2], pw[e % 2][:, :].rearrange("p (c t) -> p c t", c=2)).then_inc(u_taken, 1)
            for c in range(PH // 2):
                for t in range(TT):
                    act.wait_ge(score_done, 2 * c + t + 1)
                    copy(score[:, t * PH + 2 * c:t * PH + 2 * c + 2],
                         px[(2 * c + t) % 4][:, :].rearrange("p (h n) -> p h n", h=2)).then_inc(score_copied, 1)
            act.wait_ge(score_copied, PH)
            act.wait_ge(gt2_spilled, 16)
            with act.Fori(0, G1 // 2) as i:
                copy(s_in[:, :, :].rearrange("p a n -> p (a n)"),
                     score[:, bass.ds(i, 1)].rearrange("p a n -> p (a n)")).then_inc(s_in_ready, 1)
                for e in range(2):
                    n0 = U0 + e + 1
                    split_hi(2 * i + n0, 16 * i + 16 * (n0 // S_RAW + 1), n0)
                    act.wait_ge(piece_used, 4 * i + (2 * (U0 + e) + 2))
                    nc.scalar.activation(W[:, bass.ds(4 * i + 2 * e, 2)],
                                         pw[e][:, :].rearrange("p (j t) -> p j t", j=2), ACT.Gelu).then_inc(u_taken, 1)
                act.wait_ge(s_in_used, i + 1)
            act.wait_ge(best_ready, 1)
            nc.scalar.activation(gate[:, :, :], gate[:, :, :], ACT.Exp).then_inc(gate_exp, 1)
            for a in range(2):
                act.wait_ge(idxT_done, 1)
                copy(idx[:, a], px[2][:, a * T:(a + 1) * T]).then_inc(g_hi_taken, 1)
            act.wait_ge(x1_spilled, 16)
            with act.Fori(0, GROUPS // 2) as i:
                for e in range(2):
                    act.wait_ge(oh_used, 2 * i + (e + 3))
                    copy(W[:, 2 * G1:NK, bass.ds(8 * i + 4 * e, 4)],
                         pv[e][:, :].rearrange("p (t j) -> p j t", t=4)[:, 2 * G1:NK]).then_inc(g_hi_taken, 1)

            def gelu(q):
                nc.scalar.activation(gel[:, :], pw[0][:, :], ACT.Gelu).then_inc(u_taken, 1)

            def split_w(q, pair, used, e):
                act.wait_ge(piece_used, used + e)
                copy(ws_hi[:, e], W[:, bass.ds(2 * pair + e, 1)].rearrange("p a t -> p (a t)")).then_inc(wsplit_hi, 1)

            act.wait_ge(piece_used, 2 * (U0 + G1) + 2)
            act.wait_ge(oh_used, GROUPS + 2)
            gelu(0)
            with act.Fori(0, STEPS) as q:
                split_hi(2 * q + U2, 16 * q + 16 * (U2 // S_RAW + 1), U2)
                act.wait_ge(prod_ready, q + 1)
                for e in range(2):
                    split_w(q, q + G1, 4 * q + (2 * U2 - 1), e)
                split_hi(2 * q + (U2 + 1), 16 * q + 16 * ((U2 + 1) // S_RAW + 1), U2 + 1)
                act.wait_ge(piece_used, 4 * q + (2 * U2 + 2))
                gelu(q + 1)
            split_hi(V2, 16 * (V2 // S_RAW + 1), V2)
            act.wait_ge(prod_ready, STEPS + 1)
            for e in range(2):
                split_w(STEPS, NG - 1, 2 * V2 - 1, e)
            with act.Fori(0, G1 // 2) as i:
                for x in range(2):
                    n0 = V2 + 1 + x
                    split_hi(2 * i + n0, 16 * i + 16 * (n0 // S_RAW + 1), n0)
                    for e in range(2):
                        split_w(0, 2 * i + x, 4 * i + (2 * n0 - 1), e)
            for t in range(TT):
                act.wait_ge(var2_ready, t + 1)
                nc.scalar.activation(std[:, t:t + 1], std[:, t:t + 1], ACT.Sqrt).then_inc(std2_ready, 1)

        @block.tensor
        def _(pe):
            def three(out, pairs, start=True, stop=True):
                for x, (lh, ll, rh, rl) in enumerate(pairs):
                    nc.tensor.matmul(out, lh, rh, start=start and x == 0, stop=False)
                    nc.tensor.matmul(out, lh, rl, start=False, stop=False)
                    last = nc.tensor.matmul(out, ll, rh, start=False, stop=stop and x == len(pairs) - 1)
                return last

            def weights(m):
                s = m % S_PIECE
                return w_hi[:, s], w_lo[:, s]

            def columns_piece(m, out, act_chunk=0, chunks=KC, cols=P):
                hi, lo = (w.rearrange("p (k c) -> p k c", k=chunks) for w in weights(m))
                for c in range(cols // P):
                    q = slice(c * P, (c + 1) * P)
                    last = three(out[:, c * T:(c + 1) * T],
                                 [(hi[:, k, q], lo[:, k, q], a_hi[:, act_chunk + k], a_lo[:, act_chunk + k])
                                  for k in range(chunks)])
                last.then_inc(piece_used, 1)

            def rows_piece(b, h, x_hi, x_lo):
                hi, lo = (w.rearrange("p (k c) -> p k c", k=KC // 2) for w in weights(2 * b + h))
                for t, bk in enumerate((pw[b % 2], pv[b % 2])):
                    q = slice(t * P, (t + 1) * P)
                    last = three(bk[:, 0:256],
                                 [(x_hi[:, 4 * h + k, q], x_lo[:, 4 * h + k, q], hi[:, k], lo[:, k])
                                  for k in range(KC // 2)], start=h == 0, stop=h == 1)
                last.then_inc(piece_used, 1)

            pe.wait_ge(consts, 1)
            pe.wait_ge(ada_done, ADA_THIRD)
            for c in range(2 * KC):
                last = nc.tensor.matmul(px[0][:, c:c + 1], acc[:, 0, c * P:(c + 1) * P], ones_col[:, :],
                                        start=True, stop=True)
            last.then_inc(mod1_ready, 1)

            def after(b):
                if b == 14:
                    pe.wait_ge(qk_ready, 2)
                    pe.wait_ge(act_took, evac_count(12))
                    for t, dst in enumerate((px[3], pv[0])):
                        for h in range(HG):
                            q = slice(h * T + t * P, h * T + (t + 1) * P)
                            last = nc.tensor.matmul(dst[:, h * P:(h + 1) * P], k_e[:, q], q_e[:, q], start=True, stop=True)
                        last.then_inc(aT_done, 1)
                if b == 15:
                    pe.wait_ge(act_took, evac_count(13))
                    for t, dst in enumerate((pv[1], px[3])):
                        if t:
                            pe.wait_ge(aT_copied, 1)
                        for h in range(HG):
                            q = slice(h * T + t * P, h * T + (t + 1) * P)
                            last = nc.tensor.transpose(dst[:, h * P:(h + 1) * P], k_l[:, q], ident[:, :])
                        last.then_inc(kl_done, 1)
                if b in (16, 17):
                    for n in ((0,) if b == 16 else (1, 2)):
                        dst = (pv[0], pv[1], px[3])[n]
                        pe.wait_ge(kl_ready, n // 2 + 1)
                        pe.wait_ge(aT_copied, 2)
                        if n:
                            pe.wait_ge(kl_ready, 2)
                        t, q = n // 2, slice((n % 2) * CH, (n % 2 + 1) * CH)
                        for h in range(HG):
                            last = nc.tensor.matmul(dst[:, h * P:(h + 1) * P], kl_nat[q, t, h],
                                                    vh[q, t, h * P:(h + 1) * P], start=True, stop=True)
                        last.then_inc(ds_done, 1)
                if b == 19:
                    pe.wait_ge(aT_ready, 1)
                    pe.wait_ge(state_ready, 3)
                    for t, dst in enumerate((px[3], pv[0])):
                        for h in range(HG):
                            o = slice(h * P, (h + 1) * P)
                            for c in range(2):
                                n, r = 2 * t + c, slice(c * CH, (c + 1) * CH)
                                last = nc.tensor.matmul(dst[r, o], aT[:, t, h, r], vh[:, t, o], start=True, stop=n == 0)
                                if n:
                                    x = h * T + n * CH
                                    last = nc.tensor.matmul(dst[r, o], q_x[:, x:x + CH], state[:, n - 1, o],
                                                            start=False, stop=True)
                        last.then_inc(o_done, 1)
                h = b - 13
                if 0 <= h < HEADS:
                    pe.wait_ge(act_took, evac_count(KA + 1))
                    if h >= 1:
                        pe.wait_ge(s_max, h)
                    r = slice((h % 2) * DH, (h % 2 + 1) * DH)
                    nc.tensor.matmul(px[0][:, 0:P], qT[r, h // 2, 0:P], kT[r, h // 2, 0:P], start=True, stop=True)
                    nc.tensor.matmul(px[0][:, P:3 * P], qT[r, h // 2, P:T], kT[r, h // 2, :], start=True, stop=True) \
                        .then_inc(s_done, 1)

                def transposes(h):
                    pe.wait_ge(p_ready, h + 1)
                    if h >= 1:
                        pe.wait_ge(pT_ready, h)
                    for x in range(3):
                        last = nc.tensor.transpose(px[1][:, x * P:(x + 1) * P], prob[:, h % 2, x * P:(x + 1) * P], ident[:, :])
                    last.then_inc(pT_done, 1)

                def values(h):
                    pe.wait_ge(pT_ready, h + 1)
                    pe.wait_ge(act_took, evac_count(VA + 1))
                    if h >= 2 and h % 2 == 0:
                        pe.wait_ge(ya_copied, h // 2)
                    o, v = slice((h % 2) * DH, (h % 2 + 1) * DH), slice(h * DH, (h + 1) * DH)
                    nc.tensor.matmul(px[2][o, 0:T], va[:, 0, v], pT[:, 0:T], start=True, stop=False)
                    nc.tensor.matmul(px[2][o, P:T], va[:, 1, v], pT[:, T:3 * P], start=False, stop=True).then_inc(pv_done, 1)

                if 0 <= b - 14 < HEADS:
                    transposes(b - 14)
                if 0 <= b - 15 < HEADS - 1:
                    values(b - 15)
                if b == 21:
                    values(HEADS - 1)
                    pe.wait_ge(ada_done, ADA_TILES)
                    for half in range(2):
                        last = nc.tensor.matmul(px[half][:, :], ones_pp[:, :], acc[:, 1, half * 512:(half + 1) * 512],
                                                start=True, stop=True)
                    last.then_inc(gt1_done, 1)
                    pe.wait_ge(gt1_ready, 1)
                    for c in range(KC):
                        nc.tensor.matmul(px[0][:, c:c + 1], acc[:, 1, ADA_W + c * P:ADA_W + (c + 1) * P],
                                         ones_col[:, :], start=True, stop=True)
                    for c in range(KC):
                        last = nc.tensor.matmul(px[0][:, KC + c:KC + c + 1], acc[:, 0, c * P:(c + 1) * P],
                                                ones_col[:, :], start=True, stop=True)
                    last.then_inc(mod2_done, 1)
                    pe.wait_ge(ya_copied, HEADS // 2)
                    nc.tensor.matmul(px[1][0:1, :], ones_col[:, :], acc[:, 0, ADA_W:ADA_W + 512], start=True, stop=True)
                    nc.tensor.matmul(px[2][0:1, :], ones_col[:, :], acc[:, 0, ADA_W + 512:2 * ADA_W],
                                     start=True, stop=True).then_inc(gt2_done, 1)
                    pe.wait_ge(yb_ready, 1)
                    for t, dst in enumerate((pv[1], px[3])):
                        for c in range(HG):
                            last = nc.tensor.transpose(dst[:, c * P:(c + 1) * P], o_nat[:, t, c * P:(c + 1) * P], ident[:, :])
                        last.then_inc(ybT_done, 1)

            for b in range(NA):
                for h in range(2):
                    m = 2 * b + h
                    pe.wait_ge(lo_ready, m + 1)
                    if h == 0 and b >= 2:
                        pe.wait_ge(dve_took if b - 2 in DVE_EVAC else act_took, evac_count(b - 2))
                    if h == 0 and b == 0:
                        pe.wait_ge(act_lo, 2)
                    if b < BRANCH and b not in NATURAL:
                        columns_piece(m, pw[b % 2][:, h * T:(h + 1) * T])
                    elif b in NATURAL:
                        if b == WOUT:
                            pe.wait_ge(m_lo_ready, 2 * h + 2)
                        x_hi, x_lo = (a_hi, a_lo) if b < BRANCH else (m_hi, m_lo)
                        rows_piece(b, h, x_hi, x_lo)
                    elif b < WOUT:
                        if b == BRANCH and h == 0:
                            pe.wait_ge(act_lo, 4)
                        if b < BRANCH + 2 and h == 1:
                            pe.wait_ge(act_hi, 4)
                        columns_piece(m, (pw, pv)[h][b % 2], act_chunk=HG * h, chunks=HG, cols=2 * P)
                    else:
                        if b == WQ and h == 0:
                            for t in range(TT):
                                pe.wait_ge(x1_ready, t + 1)
                                for k in range(KC):
                                    at = (k % 2) * T + t * P
                                    last = nc.tensor.transpose(px[k // 2][:, at:at + P], x1[:, t, k * P:(k + 1) * P], ident[:, :])
                            last.then_inc(x1T_done, 1)
                            pe.wait_ge(act_lo, 6)
                        columns_piece(m, pw[b % 2][:, h * T:(h + 1) * T])
                after(b)

            pe.wait_ge(keys_landed, 32)
            for c in range(PH // 2):
                if c < 2:
                    pe.wait_ge(act_took, evac_count(WQ + c))
                else:
                    pe.wait_ge(u_taken, c - 1)
                for t in range(TT):
                    x = 2 * c + t
                    if x >= 4:
                        pe.wait_ge(score_copied, x - 3)
                    for h in range(2):
                        last = nc.tensor.matmul(px[x % 4][:, h * T:(h + 1) * T], qpT[:, 2 * c + h, t * P:(t + 1) * P],
                                                keys[:, 2 * c + h], start=True, stop=True)
                    last.then_inc(score_done, 1)

            def u_pair(n, n0, bk):
                for e in range(2):
                    pe.wait_ge(lo_ready, 2 * n + (e + 1))
                    columns_piece(2 * n0 + e, bk[:, e * T:(e + 1) * T])

            def v_pair(n, n0, split, first=False, final=False):
                for e in range(2):
                    pe.wait_ge(lo_ready, 2 * n + (e + 1))
                    pe.wait_ge(wsplit_lo, split + (e + 1))
                    hi, lo = weights(2 * n0 + e)
                    for t in range(TT):
                        q = slice(t * P, (t + 1) * P)
                        for x, (l, r) in enumerate(((ws_hi, hi), (ws_hi, lo), (ws_lo, hi))):
                            for half in range(2):
                                last = nc.tensor.matmul(px[2 * t + half][:, :], l[:, e, q], r[:, half * 512:(half + 1) * 512],
                                                        start=first and e == 0 and x == 0,
                                                        stop=final and e == 1 and x == 2)
                        if final and e == 1 and t == 0:
                            last.then_inc(y_done, 1)
                    last.then_inc(piece_used, 1)

            with pe.Fori(0, G1 // 2) as i:
                for e in range(2):
                    pe.wait_ge(u_taken, 2 * i + (e + 1))
                    u_pair(2 * i + (U0 + e), U0 + e, pw[e])
            pe.wait_ge(gate_ready, 1)
            for a, src in enumerate((ij[:, 0], ij[:, 1], gate[:, :, :])):
                for t in range(TT):
                    at = (a % 2) * T + t * P
                    last = nc.tensor.transpose(px[2 + a // 2][:, at:at + P],
                                               src[:, t * PH:(t + 1) * PH].rearrange("p h k -> p (h k)"), ident[:, :])
                last.then_inc(oh_used if a == 0 else idxT_done, 2 if a == 0 else 1)
            with pe.Fori(0, GROUPS // 2) as i:
                for e in range(2):
                    pe.wait_ge(g_lo_taken, 2 * i + (e + 1))
                    pe.wait_ge(g_hi_taken, 2 * i + (e + 1))
                    pe.wait_ge(ohi_ready, 2 * i + (e + 1))
                    pe.wait_ge(ohj_ready, 2 * i + (e + 1))
                    for tk in range(4):
                        last = nc.tensor.matmul(pv[e][:, tk * P:(tk + 1) * P], oh_i[e][:, tk], oh_j[e][:, tk],
                                                start=True, stop=True)
                    last.then_inc(oh_used, 1)
            pe.wait_ge(u_taken, G1 + 1)
            u_pair(U0 + G1, U0 + G1, pw[0])

            def step(q, first=False):
                pe.wait_ge(u_taken, q + (G1 + 3))
                u_pair(2 * q + U2, U2, pw[0])
                v_pair(2 * q + (U2 + 1), U2 + 1, 2 * q, first=first)

            step(0, first=True)
            with pe.Fori(1, STEPS) as q:
                step(q)
            v_pair(V2, V2, 2 * STEPS)
            with pe.Fori(0, G1 // 2 - 1) as i:
                for x in range(2):
                    v_pair(2 * i + (V2 + 1 + x), V2 + 1 + x, 4 * i + (2 * (STEPS + 1 + x)))
            for x in range(2):
                n = V2 + G1 - 1 + x
                v_pair(n, n, 2 * (STEPS + G1 - 1 + x), final=x == 1)

        @block.vector
        def _(dve):
            v = nc.vector

            def layer_norm_stats(z, tiles):
                for t in tiles:
                    for half in range(2):
                        i = (2 * t + half) * 6
                        last = v.bn_stats(bn[:, i:i + 6], z[:, t, half * 512:(half + 1) * 512])
                    link(last)
                    link(v.bn_aggr(mv[:, 2 * t:2 * t + 2], bn[:, 12 * t:12 * t + 12]))

            def layer_norm_apply(z, t, g, b):
                link(v.reciprocal(rstd[:, t:t + 1], std[:, t:t + 1]))
                link(v.tensor_scalar(z, z, mv[:, 2 * t:2 * t + 1], rstd[:, t:t + 1], ALU.subtract, ALU.mult))
                link(v.tensor_tensor(z, z, g[:, :], ALU.mult))
                return v.tensor_tensor(z, z, b[:, :], ALU.add)

            chain = {"n": 0, "at": None}

            def link(ins):
                chain["n"] += 1
                ins.then_inc(dve_chain, 1)
                dve.wait_ge(dve_chain, chain["n"] if chain["at"] is None else chain["at"] + chain["n"])

            def mark(ins, s, value):
                ins.then_inc(s, 1)
                dve.wait_ge(s, value)

            def split_lo_piece(n, n0, e):
                m0 = (2 * n0 + e) % S_PIECE
                dve.wait_ge(hi_ready, 2 * n + (e + 1))
                v.tensor_tensor(w_lo[:, m0], raw[:, n0 % S_RAW, e], w_hi[:, m0].bitcast(F32), ALU.subtract).then_inc(lo_ready, 1)

            def split_lo(n, n0):
                for e in range(2):
                    split_lo_piece(n, n0, e)

            def sum_ada(t):
                third, k, half = ada_tile(t)
                if t % ADA_THIRD == 0:
                    dve.wait_ge(bias_landed[third], 16)
                dve.wait_ge(ada_landed[t % ADA_SLOTS], 16 * (t // ADA_SLOTS + 1))
                if t >= 2:
                    dve.wait_ge(ada_done, t - 1)
                a = acc[:, third % 2, half * ADA_W:(half + 1) * ADA_W]
                v.scalar_tensor_tensor(a, ada[:, t % ADA_SLOTS], sc_col[:, k:k + 1], a, ALU.mult, ALU.add).then_inc(ada_done, 1)

            dve.wait_ge(small_landed, 32)
            link(v.tensor_tensor(lb_max[:, :], lb_raw[:, 0:HG], lb_raw[:, HG:2 * HG], ALU.max))
            mark(v.tensor_tensor(lb_e[:, :].rearrange("p (a h) -> p a h", a=2), lb_raw[:, :].rearrange("p (a h) -> p a h", a=2),
                                 lb_max[:, :].unsqueeze(1).broadcast_to([P, 2, HG]), ALU.subtract), lb_max_ready, 1)
            dve.wait_ge(lb_e_ready, 1)
            link(v.tensor_tensor(lb_max[:, :], lb_e[:, 0:HG], lb_e[:, HG:2 * HG], ALU.add))
            link(v.reciprocal(lb_max[:, :], lb_max[:, :]))
            link(v.tensor_tensor(lb_col[:, :], lb_e[:, 0:HG], lb_max[:, :], ALU.mult))
            link(v.tensor_scalar(om_lb[:, :], lb_col[:, :], -1.0, 1.0, ALU.mult, ALU.add))
            dve.wait_ge(c_sig_ready, 1)
            link(v.tensor_tensor(sc_col[:, :], c_col[:, :], c_sig[:, :], ALU.mult))
            for t in range(ADA_THIRD):
                sum_ada(t)
            dve.wait_ge(mod1_ready, 1)
            v.tensor_copy(mod1[:, 0:KC], px[0][:, 0:KC])
            link(v.tensor_scalar(mod1[:, KC:2 * KC], px[0][:, KC:2 * KC], 1.0, None, ALU.add))
            dve.wait_ge(xT_landed, 16)
            for k in range(KC):
                ins = v.tensor_scalar(xT[:, k], xT[:, k], mod1[:, KC + k:KC + k + 1], mod1[:, k:k + 1], ALU.mult, ALU.add)
                if k % 4 == 3:
                    mark(ins, h_ready, k // 4 + 1)

            def act_split_lo(src, stage):
                for half in range(2):
                    q = slice(half * KC // 2, (half + 1) * KC // 2)
                    dve.wait_ge(act_hi, stage + half + 1)
                    v.tensor_tensor(a_lo[:, q], src[:, q], a_hi[:, q].bitcast(F32), ALU.subtract).then_inc(act_lo, 1)

            for b in range(NA):
                split_lo(b, b)
                if b == 1:
                    act_split_lo(xT, 0)
                e = b - 2
                s = e % 2
                if HQ <= e < HQ + 2:
                    r = slice((e - HQ) * 512, (e - HQ + 1) * 512)
                    dve.wait_ge(sig_done, e - HQ + 1)
                    v.tensor_tensor(qh[:, r], pw[s][:, :], qh[:, r], ALU.mult).then_inc(dve_took, 1)
                if HGATE <= e < HGATE + 2:
                    r = e - HGATE
                    dve.wait_ge(sig_done, r + 3)
                    for t, src in enumerate((pw[s], pv[s])):
                        d = sgh[:, t, r * 256:(r + 1) * 256]
                        last = v.tensor_tensor(d, src[:, 0:256], d, ALU.mult)
                    last.then_inc(dve_took, 1)
                h = b - 15
                if 0 <= h < HEADS:
                    x = h % 2
                    dve.wait_ge(s_done, h + 1)
                    if h == 0:
                        dve.wait_ge(consts, 3)
                    if h >= 2:
                        dve.wait_ge(pT_done, h - 1)
                    link(v.scalar_tensor_tensor(prob[:, x], dist[:, :], -(2.0 ** (-8.0 * (h + 1) / HEADS)), px[0][:, 0:3 * P],
                                                ALU.mult, ALU.add))
                    v.reduce_max(rmax[:, 2 * x:2 * x + 1], prob[:, x, 0:P], AX)
                    link(v.reduce_max(rmax[:, 2 * x + 1:2 * x + 2], prob[:, x, P:3 * P], AX))
                    mark(v.tensor_scalar(rmax[:, 2 * x:2 * x + 2], rmax[:, 2 * x:2 * x + 2], -1.0, None, ALU.mult), s_max, h + 1)
                if b == 4:
                    dve.wait_ge(act_took, evac_count(HF + 1))
                    for c in range(HG):
                        q = slice(c * T, (c + 1) * T)
                        last = v.tensor_scalar(lf[:, q], lf[:, q], om_lb[:, c:c + 1], lb_col[:, c:c + 1], ALU.mult, ALU.add)
                    link(last)
                    v.tensor_scalar(kh[:, :], lf[:, :], -1.0, 1.0, ALU.mult, ALU.add).then_inc(f_ready, 1)
                if b == 10:
                    dve.wait_ge(lf_ready, 1)
                    dve.wait_ge(consts, 5)
                    link(v.tensor_tensor_scan(bcum[:, :], scan_m[:, :], lf[:, :], 0.0, ALU.mult, ALU.add))
                    bc = bcum[:, :].rearrange("p (n c) -> p n c", c=CH)
                    full = [P, HG * NCH, CH]
                    v.tensor_tensor(q_e[:, :].rearrange("p (n c) -> p n c", c=CH), bc,
                                    bc[:, :, CH // 2:CH // 2 + 1].broadcast_to(full), ALU.subtract).then_inc(d_ready, 1)
                    v.tensor_tensor(k_l[:, :].rearrange("p (n c) -> p n c", c=CH),
                                    bc[:, :, CH - 1:CH].broadcast_to(full), bc, ALU.subtract).then_inc(d_ready, 1)
                if b == 12:
                    dve.wait_ge(e_ready, 1)
                    v.tensor_tensor(k_e[:, :], k_e[:, :], kh[:, :], ALU.mult)
                    v.tensor_tensor(q_e[:, :], q_e[:, :], qh[:, :], ALU.mult).then_inc(qk_ready, 1)
                if b == 13:
                    v.tensor_tensor(k_l[:, :], k_l[:, :], kh[:, :], ALU.mult)
                    v.tensor_tensor(q_x[:, :], q_x[:, :], qh[:, :], ALU.mult).then_inc(qk_ready, 1)
                for n in range(NCH - 1):
                    if b == (18, 19, 19)[n]:
                        dve.wait_ge(ds_done, n + 1)
                        src = (pv[0], pv[1], px[3])[n]
                        if n == 0:
                            mark(v.tensor_copy(state[:, 0], src[:, :]), state_ready, 1)
                        else:
                            dec = decay[:, :].rearrange("p (h n) -> p h n", n=NCH)[:, :, n:n + 1].broadcast_to([P, HG, P])
                            link(v.tensor_tensor(state[:, n].rearrange("p (h d) -> p h d", h=HG),
                                                 state[:, n - 1].rearrange("p (h d) -> p h d", h=HG), dec, ALU.mult))
                            mark(v.tensor_tensor(state[:, n], state[:, n], src[:, :], ALU.add), state_ready, n + 1)
                if b == 21:
                    sq = qh[:, :].rearrange("p (a n) -> p a n", a=TT)
                    for t in range(TT):
                        dve.wait_ge(o_copied, t + 1)
                        last = v.tensor_tensor(sq[:, t], o_nat[:, t], o_nat[:, t], ALU.mult)
                    link(last)
                    link(v.tensor_reduce(sumsq[:, :], qh[:, :].rearrange("p (g d) -> p g d", d=P), AX, ALU.add))
                    v.tensor_scalar(sumsq[:, :], sumsq[:, :], 1.0 / P, RMS_EPS, ALU.mult, ALU.add).then_inc(ss_ready, 1)
                    dve.wait_ge(rms_ready, 1)
                    link(v.reciprocal(rms_i[:, :], rms[:, :]))
                    dve.wait_ge(norm_landed, 16)
                    ov = o_nat[:, :, :].rearrange("p a (h d) -> p (a h) d", d=P)
                    link(v.tensor_tensor(ov, ov, rms_i[:, :].unsqueeze(2).broadcast_to([P, TT * HG, P]), ALU.mult))
                    link(v.tensor_tensor(o_nat[:, :, :], o_nat[:, :, :], norm_g[:, :].unsqueeze(1).broadcast_to([P, TT, HG * P]), ALU.mult))
                    v.tensor_tensor(o_nat[:, :, :], o_nat[:, :, :], sgh[:, :, :], ALU.mult).then_inc(yb_ready, 1)
                h = b - 15
                if 0 <= h < HEADS:
                    x = h % 2
                    dve.wait_ge(p_exp, h + 1)
                    link(v.reciprocal(rinv[:, 2 * x:2 * x + 2], rsum[:, 2 * x:2 * x + 2]))
                    v.tensor_scalar(prob[:, x, 0:P], prob[:, x, 0:P], rinv[:, 2 * x:2 * x + 1], None, ALU.mult)
                    v.tensor_scalar(prob[:, x, P:3 * P], prob[:, x, P:3 * P], rinv[:, 2 * x + 1:2 * x + 2], None,
                                    ALU.mult).then_inc(p_ready, 1)
                for t in ada_at(b):
                    sum_ada(t)
                if b == 23:
                    dve.wait_ge(gt1_done, 1)
                    v.tensor_copy(gt1[:, 0:512], px[0][:, :])
                    v.tensor_copy(gt1[:, 512:1024], px[1][:, :]).then_inc(gt1_ready, 1)
                    dve.wait_ge(act_hi, 3)
                    v.tensor_tensor(a_lo[:, 0:4], yaT[:, :, :], a_hi[:, 0:4].bitcast(F32), ALU.subtract).then_inc(act_lo, 1)
                    dve.wait_ge(act_hi, 4)
                    for t, src in enumerate((pv[1], px[3])):
                        q = slice(t * P, (t + 1) * P)
                        last = v.tensor_tensor(a_lo[:, 4:8, q], src[:, :].rearrange("p (h t) -> p h t", h=HG),
                                               a_hi[:, 4:8, q].bitcast(F32), ALU.subtract)
                    last.then_inc(act_lo, 1)
                    dve.wait_ge(mod2_done, 1)
                    v.tensor_copy(mod2[:, 0:KC], px[0][:, 0:KC])
                    link(v.tensor_scalar(mod2[:, KC:2 * KC], px[0][:, KC:2 * KC], 1.0, None, ALU.add))
                    dve.wait_ge(gt2_done, 1)
                    v.tensor_copy(gt2_row[0:1, 0:512], px[1][0:1, :])
                    v.tensor_copy(gt2_row[0:1, 512:1024], px[2][0:1, :]).then_inc(gt2_ready, 1)
                if BRANCH <= e < BRANCH + 4:
                    r = e - BRANCH
                    q = slice(2 * r, 2 * r + 2)
                    dve.wait_ge(gates_ready, 1)
                    dve.wait_ge(piece_used, 2 * e + 2)
                    if r >= 1:
                        dve.wait_ge(m_hi_ready, r)
                    v.tensor_tensor(br_a[:, :], pw[s][:, :], sig_a[:, q].rearrange("p c t -> p (c t)"), ALU.mult)
                    ins = v.tensor_tensor(br_b[:, :], pv[s][:, :], sig_b[:, q].rearrange("p c t -> p (c t)"), ALU.mult)
                    mark(ins, dve_took, evac_count(e))
                    mark(v.tensor_tensor(mix[:, :], br_a[:, :], br_b[:, :], ALU.add), mix_ready, r + 1)
                    dve.wait_ge(m_hi_ready, r + 1)
                    mark(v.tensor_tensor(m_lo[:, q].rearrange("p c t -> p (c t)"), mix[:, :],
                                         m_hi[:, q].rearrange("p c t -> p (c t)").bitcast(F32), ALU.subtract), m_lo_ready, r + 1)
                if WOUT <= e < WQ:
                    r = e - WOUT
                    q = slice(r * 256, (r + 1) * 256)
                    dve.wait_ge(piece_used, 2 * e + 2)
                    if r == 0:
                        dve.wait_ge(x_landed, 48)
                    for t, src in enumerate((pw[s], pv[s])):
                        last = v.tensor_tensor(x1[:, t, q], src[:, 0:256], gt1[:, q], ALU.mult)
                    mark(last, dve_took, evac_count(e))
                    for t in range(TT):
                        last = v.scalar_tensor_tensor(x1[:, t, q], x_nat[:, t, q], ALPHA, x1[:, t, q], ALU.mult, ALU.add)
                    link(last)
                    if r == 3:
                        layer_norm_stats(x1, range(TT))
                        v.tensor_scalar(std[:, :], mv[:, :].rearrange("p (t x) -> p t x", x=2)[:, :, 1], LN_EPS, None,
                                        ALU.add).then_inc(var_ready, 1)
                        dve.wait_ge(std_ready, 1)
                        for t in range(TT):
                            layer_norm_apply(x1[:, t], t, ln1_g, ln1_b).then_inc(x1_ready, 1)
                        dve.wait_ge(x1T_done, 1)
                        for k in range(KC):
                            ins = v.tensor_scalar(h2f[:, k], px[k // 2][:, (k % 2) * T:(k % 2 + 1) * T],
                                                  mod2[:, KC + k:KC + k + 1], mod2[:, k:k + 1], ALU.mult, ALU.add)
                            if k % 4 == 3:
                                mark(ins, h2f_ready, k // 4 + 1)
                        act_split_lo(h2f, 4)

            split_lo(U0, U0)
            iota16 = iota[:, 0:TOPK]

            def go(ins):
                chain["n"] += 1
                ins.then_inc(dve_chain, 1)
                return chain["n"]

            def need(c, alone=False):
                dve.wait_ge(dve_chain, chain["at"] + c)
                if alone:
                    v.nop(nofuse=True)

            start, per_unit = chain["n"], 22
            with dve.Fori(0, G1 // 2) as i:
                chain["at"], chain["n"] = per_unit * i + start, 0
                dve.wait_ge(s_in_ready, i + 1)
                v.nop(nofuse=True)
                first = [go(v.max(top_v[:, a, 0:8], s_in[:, a])) for a in range(2)]
                cut = []
                for a in range(2):
                    need(first[a], alone=True)
                    v.max_index(top_i[:, a, 0:8], top_v[:, a, 0:8], s_in[:, a])
                    cut.append(go(v.match_replace(s_cut[:, a], top_v[:, a, 0:8], s_in[:, a], NEG)))
                second = []
                for a in range(2):
                    need(cut[a], alone=True)
                    second.append(go(v.max(top_v[:, a, 8:16], s_cut[:, a])))
                for a in range(2):
                    need(second[a], alone=True)
                    found = go(v.max_index(top_i[:, a, 8:16], top_v[:, a, 8:16], s_cut[:, a]))
                made = go(v.tensor_tensor(cand[:, :, :], top_v[:, 0].unsqueeze(2).broadcast_to([P, TOPK, TOPK]),
                                          top_v[:, 1].unsqueeze(1).broadcast_to([P, TOPK, TOPK]), ALU.add))
                need(found)
                named = go(v.tensor_copy(top_f[:, :, :], top_i[:, :, :]))
                split_lo_piece(2 * i + (U0 + 1), U0 + 1, 0)
                flat = cand[:, :, :].rearrange("p a b -> p (a b)")
                need(made, alone=True)
                first = go(v.max(best_t[:, 0:8], flat))
                split_lo_piece(2 * i + (U0 + 1), U0 + 1, 1)
                need(first, alone=True)
                v.max_index(pos[:, 0:8], best_t[:, 0:8], flat)
                cut = go(v.match_replace(c_cut[:, :], best_t[:, 0:8], flat, NEG))
                need(cut, alone=True)
                second = go(v.max(best_t[:, 8:16], c_cut[:, :]))
                split_lo_piece(2 * i + (U0 + 2), U0 + 2, 0)
                need(second, alone=True)
                found = go(v.max_index(pos[:, 8:16], best_t[:, 8:16], c_cut[:, :]))
                v.tensor_copy(best[:, bass.ds(i, 1)].rearrange("p a k -> p (a k)"), best_t[:, :])
                need(found)
                v.tensor_single_scalar(pos2[:, 0], pos[:, :], 4, op=ALU.logical_shift_right)
                halves = go(v.tensor_single_scalar(pos2[:, 1], pos[:, :], TOPK - 1, op=ALU.bitwise_and))
                need(halves)
                places = go(v.tensor_copy(posf[:, :, :], pos2[:, :, :]))
                split_lo_piece(2 * i + (U0 + 2), U0 + 2, 1)
                need(places)
                hit = [go(v.tensor_tensor(eq[:, a], posf[:, a].unsqueeze(2).broadcast_to([P, TOPK, TOPK]),
                                          iota16.unsqueeze(1).broadcast_to([P, TOPK, TOPK]), ALU.is_equal)) for a in range(2)]
                need(named)
                key = []
                for a in range(2):
                    need(hit[a])
                    key.append(go(v.tensor_tensor(eq[:, a], eq[:, a], top_f[:, a].unsqueeze(1).broadcast_to([P, TOPK, TOPK]),
                                                  ALU.mult)))
                for a in range(2):
                    need(key[a])
                    last = go(v.tensor_reduce(ij[:, a, bass.ds(i, 1)].rearrange("p a k -> p (a k)"), eq[:, a], AX, ALU.add))
                need(last)
                v.tensor_copy(best_t[:, 0:1], best_t[:, 0:1]).then_inc(s_in_used, 1)
                assert chain["n"] == per_unit, chain["n"]
            chain["at"], chain["n"] = None, start + per_unit * (G1 // 2)
            link(v.tensor_tensor(gate[:, :, :], best[:, :, :], best[:, :, 0:1].broadcast_to([P, TT * PH, TOPK]), ALU.subtract))
            mark(v.tensor_copy(mv[:, 0:1], mv[:, 0:1]), best_ready, 1)
            dve.wait_ge(gate_exp, 1)
            link(v.tensor_reduce(gsum[:, :], gate[:, :, :], AX, ALU.add))
            link(v.reciprocal(ginv[:, :], gsum[:, :]))
            v.tensor_tensor(gate[:, :, :], gate[:, :, :], ginv[:, :].unsqueeze(2).broadcast_to([P, TT * PH, TOPK]),
                            ALU.mult).then_inc(gate_ready, 1)
            for t in range(TT):
                dve.wait_ge(idxT_done, 2)
                v.tensor_copy(idx[:, 2, t * P:(t + 1) * P], px[3][:, t * P:(t + 1) * P]).then_inc(g_lo_taken, 1)
            dve.wait_ge(g_hi_taken, 2)
            dve.wait_ge(g_lo_taken, 2)

            def one_hot(i, e):
                dve.wait_ge(oh_used, 2 * i + (e + 1))
                for y in range(4):
                    t = 8 * i + (4 * e + y)
                    if y < 3:
                        v.tensor_scalar(oh_j[e][:, y], iota[:, :], idx[:, 1, bass.ds(t, 1)], None, ALU.is_equal)
                    last = v.tensor_scalar(oh_i[e][:, y], iota[:, :], idx[:, 0, bass.ds(t, 1)],
                                           idx[:, 2, bass.ds(t, 1)], ALU.is_equal, ALU.mult)
                last.then_inc(ohi_ready, 1)

            def take(i, e):
                dve.wait_ge(g_hi_taken, 2 * i + (e + 3))
                w = W[:, 0:2 * G1, bass.ds(8 * i + 4 * e, 4)]
                v.tensor_tensor(w, pv[e][:, :].rearrange("p (t j) -> p j t", t=4)[:, 0:2 * G1], w, ALU.mult).then_inc(g_lo_taken, 1)

            one_hot(0, 0)
            with dve.Fori(0, GROUPS // 2 - 1) as i:
                one_hot(i, 1)
                take(i, 0)
                one_hot(i + 1, 0)
                take(i, 1)
            i = GROUPS // 2 - 1
            one_hot(i, 1)
            take(i, 0)
            take(i, 1)

            def product(q):
                dve.wait_ge(u_taken, q + (G1 + 3))
                w = W[:, bass.ds(2 * q + 2 * G1, 2)].rearrange("p a t -> p (a t)")
                v.tensor_tensor(w, w, gel[:, :], ALU.mult).then_inc(prod_ready, 1)

            def w_lo_part(pair, split, e):
                dve.wait_ge(wsplit_hi, split + (e + 1))
                v.tensor_tensor(ws_lo[:, e], W[:, bass.ds(2 * pair + e, 1)].rearrange("p a t -> p (a t)"),
                                ws_hi[:, e].bitcast(F32), ALU.subtract).then_inc(wsplit_lo, 1)

            dve.wait_ge(g_hi_taken, GROUPS + 2)
            product(0)
            with dve.Fori(0, STEPS) as q:
                split_lo(2 * q + U2, U2)
                for e in range(2):
                    w_lo_part(q + G1, 2 * q, e)
                split_lo(2 * q + (U2 + 1), U2 + 1)
                product(q + 1)
            split_lo(V2, V2)
            for e in range(2):
                w_lo_part(NG - 1, 2 * STEPS, e)
            with dve.Fori(0, G1 // 2) as i:
                for x in range(2):
                    n0 = V2 + 1 + x
                    split_lo(2 * i + n0, n0)
                    for e in range(2):
                        w_lo_part(2 * i + x, 4 * i + 2 * (STEPS + 1 + x), e)
            dve.wait_ge(end_landed, 64)
            for t in range(TT):
                if t == 0:
                    dve.wait_ge(y_done, 1)
                else:
                    dve.wait_ge(piece_used, 2 * (V2 + G1) + 2)
                for half in range(2):
                    q = slice(half * 512, (half + 1) * 512)
                    last = v.tensor_tensor(z2[:, t, q], px[2 * t + half][:, :], gt2_b[:, q], ALU.mult)
                link(last)
                link(v.scalar_tensor_tensor(z2[:, t], x1_b[:, t], ALPHA, z2[:, t], ALU.mult, ALU.add))
                layer_norm_stats(z2, [t])
                v.tensor_scalar(std[:, t:t + 1], mv[:, 2 * t + 1:2 * t + 2], LN_EPS, None, ALU.add).then_inc(var2_ready, 1)
                dve.wait_ge(std2_ready, t + 1)
                layer_norm_apply(z2[:, t], t, ln2_g, ln2_b).then_inc(z2_ready, 1)


def kernel(**inputs):
    import numpy as np
    import concourse.bacc as bacc
    from concourse.bass_utils import run_bass_kernel_spmd

    a = {k: np.asarray(x) for k, x in inputs.items()}

    def columns(w):
        n = w.shape[1] // 256
        return w.reshape(KC, P, n, 2, P).transpose(2, 1, 3, 0, 4).reshape(n, P, 2048)

    def rows(w):
        n = w.shape[1] // 256
        return w.reshape(KC, P, n, 256).transpose(2, 1, 0, 3).reshape(n, P, 2048)

    w_in = a["w_in"][0]
    cuts = np.cumsum([512] * 7 + [1024])
    qa, ka, va, hq, hf, hi, hg, ga, gb = np.split(w_in, cuts, axis=1)
    br = [a[k][0].reshape(HG, P, 4, 256).transpose(2, 1, 0, 3).reshape(4, P, 1, 1024) for k in ("w_branch_a", "w_branch_b")]
    ws = np.concatenate([columns(hf), columns(hq), rows(hi), rows(hg), columns(qa), columns(ka), rows(va),
                         columns(ga), columns(gb), np.concatenate(br, axis=2).reshape(4, P, 2048),
                         rows(a["w_out"][0]), columns(a["peer_wq"][0])])
    u = a["peer_u"][0].reshape(P, NG, 2, KC, P).transpose(1, 4, 2, 3, 0).reshape(NG, P, 2048)
    v = a["peer_v"][0].reshape(P, NG, 2 * D).transpose(1, 0, 2)
    arrays = {
        "xT": a["x"][0].T, "x": a["x"][0], "c": a["c"][0].reshape(KC, P).T, "w_ada": a["w_ada"][0], "b_ada": a["b_ada"],
        "ws": ws, "lb": a["hgrn_lb"].reshape(2, HG, P).transpose(2, 0, 1).reshape(P, 2 * HG),
        "norm_g": a["hgrn_norm_g"][0], "ln1_g": a["ln1_g"][0], "ln1_b": a["ln1_b"][0],
        "keys": a["peer_subkeys"][0].transpose(1, 3, 0, 2).reshape(P, PH, NK),
        "u": u, "v": v, "ln2_g": a["ln2_g"][0], "ln2_b": a["ln2_b"][0],
    }
    arrays = {"in_" + k: np.ascontiguousarray(x) for k, x in arrays.items()}
    nc = bacc.Bacc("TRN2", target_bir_lowering=False, num_devices=1)
    args = [nc.dram_tensor(k, x.shape, mybir.dt.from_np(x.dtype), kind="ExternalInput").ap() for k, x in arrays.items()]
    args.append(nc.dram_tensor("x1_spill", (T, D), F32).ap())
    args.append(nc.dram_tensor("gate2_spill", (1, D), F32).ap())
    args.append(nc.dram_tensor("out_0", (T, D), F32, kind="ExternalOutput").ap())
    layer(nc, *args)
    r = run_bass_kernel_spmd(nc, [arrays], core_ids=[0])
    return r.results[0]["out_0"].reshape(1, T, D)
```

```python
from contextlib import ExitStack

import concourse.bass as bass
from concourse import mybir

P = 128
F32 = mybir.dt.float32
F32R = mybir.dt.float32r
U32 = mybir.dt.uint32
I32 = mybir.dt.int32
ALU = mybir.AluOpType
ACT = mybir.ActivationFunctionType
AX = mybir.AxisListType.X

T = 256
TT = T // P
D = 1024
KC = D // P
HEADS = 8
DH = 64
HG = 4
CH = 64
NCH = T // CH
NK = 128
PH = 8
TOPK = 16
ALPHA = 2.0 ** 0.25
LN_EPS = 1e-5
RMS_EPS = 1e-6
NEG = -3.0e38
FAR = 1.0e30

HF, HQ, HI, HGATE, QA, KA, VA, GA, GB = 0, 2, 4, 6, 8, 10, 12, 14, 18
BRANCH, WOUT, WQ, NA = 22, 26, 30, 34
NATURAL = set(range(HI, HI + 2)) | set(range(HGATE, HGATE + 2)) | set(range(VA, VA + 2)) | set(range(WOUT, WQ))
DVE_EVAC = set(range(HQ, HQ + 2)) | set(range(HGATE, HGATE + 2)) | set(range(BRANCH, WQ))
NG = NK // 2
G1 = NG // 2
U0 = NA
U2 = U0 + G1 + 1
STEPS = NG - 1 - G1
V2 = U2 + 2 * STEPS
S_RAW, S_PIECE = 2, 4
S_OH = 4
POOL_LO = range(4, 24)
GROUPS = T // 4

ADA_W, ADA_SLOTS = 1024, 4
ADA_TILES = 6 * D // ADA_W * KC
ADA_THIRD = ADA_TILES // 3


def ada_tile(t):
    third, r = divmod(t, ADA_THIRD)
    k, half = (r % KC, r // KC) if third == 0 else divmod(r, 2)
    return third, k, half


def evac_count(b):
    mine = b in DVE_EVAC
    return sum(1 for x in range(b + 1) if (x in DVE_EVAC) == mine)


def ada_at(b):
    first = ADA_THIRD
    out = []
    for x in range(2, BRANCH + 3):
        n = 0 if x == 21 else 2 if x % 2 == 0 and x < 22 else 1
        if x == b:
            out = list(range(first, first + n))
        first += n
    assert first == ADA_TILES
    return out


def layer(nc, xT_d, x_d, c_d, w_ada_d, b_ada_d, ws_d, lb_d, norm_g_d, ln1_g_d, ln1_b_d, ln1_cols_d,
          keys_d, u_d, v_d, ln2_g_d, ln2_b_d, x1_d, gt2_d, out_d):
    with ExitStack() as ctx:
        base = nc.sbuf_base + (-nc.sbuf_base) % 64

        def sb(name, at, shape, dt=F32):
            return nc.alloc_sbuf_tensor_at(name, [P] + list(shape), dt, offset=base + 4 * at)

        def sem(name):
            return ctx.enter_context(nc.semaphore(name))

        raw = sb("raw", 0, [S_RAW, 2, 1024])
        w_hi = sb("w_hi", 4096, [S_PIECE, 1024], F32R)
        w_lo = sb("w_lo", 8192, [S_PIECE, 1024], F32R)
        a_hi = sb("a_hi", 12288, [KC, T], F32R)
        a_lo = sb("a_lo", 14336, [KC, T], F32R)
        SM, AR = 16384, 17408
        small_at = [SM]

        def small(name, n, dt=F32):
            at = small_at[0]
            small_at[0] += -(-n // 8) * 8
            assert small_at[0] <= AR
            return sb(name, at, [n], dt)

        ident = small("ident", P)
        iota = small("iota", P)
        c_col = small("c_col", KC)
        c_sig = small("c_sig", KC)
        sc_col = small("sc_col", KC)
        ones_col = small("ones_col", 1)
        ones_pp = small("ones_pp", P)
        j_col = small("j_col", 2 * S_OH)
        lb_raw = small("lb_raw", 2 * HG)
        lb_max = small("lb_max", HG)
        lb_e = small("lb_e", 2 * HG)
        lb_col = small("lb_col", HG)
        om_lb = small("om_lb", HG)
        mod1 = small("mod1", 2 * KC)
        mod2 = small("mod2", 2 * KC)
        decay = small("decay", HG * NCH)
        rmax = small("rmax", 2 * TT)
        rsum = small("rsum", 2 * TT)
        rinv = small("rinv", 2 * TT)
        sumsq = small("sumsq", TT * HG)
        rms = small("rms", TT * HG)
        rms_i = small("rms_i", TT * HG)
        ln_cols = small("ln_cols", 2 * KC)
        sb_cols = small("sb_cols", KC)
        warm = small("warm", 1)
        bn = small("bn", TT * 4 * 6)
        mv = small("mv", TT * 2)
        std = small("std", TT)
        rstd = small("rstd", TT)
        gsum = small("gsum", TT * PH)
        ginv = small("ginv", TT * PH)
        lf = sb("lf", AR + 0, [HG * T])
        o_nat = sb("o_nat", AR + 0, [TT, HG * P])
        bcum = sb("bcum", AR + 1024, [HG * T])
        kl_nat = sb("kl_nat", AR + 1024, [TT, HG, P])
        qh = sb("qh", AR + 2048, [HG * T])
        kh = sb("kh", AR + 3072, [HG * T])
        q_e = sb("q_e", AR + 4096, [HG * T])
        k_e = sb("k_e", AR + 5120, [HG * T])
        k_l = sb("k_l", AR + 6144, [HG * T])
        q_x = sb("q_x", AR + 7168, [HG * T])
        vh = sb("vh", AR + 8192, [TT, HG * P])
        sgh = sb("sgh", AR + 9216, [TT, HG * P])
        aT = sb("aT", AR + 10240, [TT, HG, P])
        state = sb("state", AR + 11264, [NCH - 1, HG * P])
        qT = sb("qT", AR + 12800, [HG, T])
        kT = sb("kT", AR + 13824, [HG, T])
        va = sb("va", AR + 14848, [TT, HEADS * DH])
        prob = sb("prob", AR + 15872, [2, 3 * P])
        pT = sb("pT", AR + 16640, [3 * P])
        dist = sb("dist", AR + 17024, [3 * P])
        xT = sb("xT", AR + 17408, [KC, T])
        sig_a = sb("sig_a", AR + 17408, [KC, T])
        sig_b = sb("sig_b", AR + 19456, [KC, T])
        ada = sb("ada", AR + 21504, [ADA_SLOTS, ADA_W])
        acc = sb("acc", AR + 25600, [2, 2 * ADA_W])
        x_nat = sb("x_nat", AR + 12800, [TT, D])
        ln1_g = sb("ln1_g", AR + 14848, [D])
        ln1_b = sb("ln1_b", AR + 10240, [D])
        norm_g = sb("norm_g", AR + 29696, [HG * P])
        scan_m = sb("scan_m", AR + 30208, [HG * T])
        m_hi = sb("m_hi", AR + 30208, [KC, T], F32R)
        m_lo = sb("m_lo", AR + 32256, [KC, T], F32R)
        yaT = sb("yaT", AR + 34304, [HG, T])
        gt1 = sb("gt1", AR + 4096, [D])
        gt2_row = sb("gt2_row", AR + 5120, [D])
        br_a = sb("br_a", AR + 6144, [2 * T])
        br_b = sb("br_b", AR + 6656, [2 * T])
        mix = sb("mix", AR + 7168, [2 * T])
        x1 = sb("x1", AR + 8192, [TT, D])
        h2f = sb("h2f", AR + 20480, [KC, T])
        score = sb("score", AR + 16384, [TT * PH, 2 * NK])
        qpT = sb("qpT", AR + 20480, [PH, T])
        keys = sb("keys", AR + 27648, [PH, 2 * NK])
        R0 = AR + 29696
        s_in = sb("s_in", R0, [2, NK])
        s_cut = sb("s_cut", R0 + 256, [2, NK])
        cand = sb("cand", R0 + 512, [TOPK, TOPK])
        c_cut = sb("c_cut", R0 + 768, [TOPK * TOPK])
        eq = sb("eq", R0 + 1024, [2, TOPK, TOPK])
        top_v = sb("top_v", R0 + 1536, [2, TOPK])
        top_i = sb("top_i", R0 + 1568, [2, TOPK], U32)
        top_f = sb("top_f", R0 + 1600, [2, TOPK])
        pos = sb("pos", R0 + 1632, [TOPK], U32)
        pos2 = sb("pos2", R0 + 1648, [2, TOPK], U32)
        posf = sb("posf", R0 + 1680, [2, TOPK])
        best = sb("best", R0 + 1712, [TT * PH, TOPK])
        gate = sb("gate", R0 + 1968, [TT * PH, TOPK])
        ij = sb("ij", R0 + 2224, [2, TT * PH, TOPK])
        best_t = sb("best_t", R0 + 2736, [TOPK])
        assert R0 + 2736 + TOPK <= AR + 32768
        W = sb("W", AR, [NK, T])
        ws_hi = sb("ws_hi", AR + 32768, [2, T], F32R)
        ws_lo = sb("ws_lo", AR + 33280, [2, T], F32R)
        OH3 = 4096 + (2 * U2 % S_PIECE) * 1024
        oh_at = [AR + 33792, AR + 32768, OH3, OH3 + 1024]
        oh_i = [sb(f"oh_i{k}", at, [4, P]) for k, at in enumerate(oh_at)]
        oh_j = [sb(f"oh_j{k}", at + 512, [4, P]) for k, at in enumerate(oh_at)]
        idx = sb("idx", AR + 34816, [3, T])
        gel = sb("gel", AR + 33792, [2 * T])
        assert base + 4 * (AR + 34816 + 768) <= nc.sbuf_usable_end
        E0 = AR + NG * T
        x1_b = sb("x1_b", E0, [TT, D])
        gt2_b = sb("gt2_b", E0 + 2048, [D])
        ln2_g = sb("ln2_g", E0 + 3072, [D])
        ln2_b = sb("ln2_b", E0 + 4096, [D])
        z2 = sb("z2", E0 + 5120, [TT, D])

        def bank(name):
            return ctx.enter_context(nc.psum_tensor(name, [P, 512], F32))

        pw = [bank("pw0"), bank("pw1")]
        pv = [bank("pv0"), bank("pv1")]
        px = [bank("px0"), bank("px1"), bank("px2"), bank("px3")]
        pg = [pv[0], pv[1], px[0], px[1]]

        raw_landed = [sem("raw_landed0"), sem("raw_landed1")]
        hi_ready, lo_ready = sem("hi_ready"), sem("lo_ready")
        piece_used = sem("piece_used")
        act_took, dve_took = sem("act_took"), sem("dve_took")
        small_landed, xT_landed, norm_landed = sem("small_landed"), sem("xT_landed"), sem("norm_landed")
        bias_landed = [sem(f"bias_landed{g}") for g in range(3)]
        ada_landed = [sem(f"ada_landed{s}") for s in range(ADA_SLOTS)]
        ada_done = sem("ada_done")
        acc_cleared = sem("acc_cleared")
        consts = sem("consts")
        pool_chain, dve_chain, act_chain = sem("pool_chain"), sem("dve_chain"), sem("act_chain")
        lb_e_ready, c_sig_ready, lb_max_ready = sem("lb_e_ready"), sem("c_sig_ready"), sem("lb_max_ready")
        mod1_ready, h_ready = sem("mod1_ready"), sem("h_ready")
        act_hi, act_lo = sem("act_hi"), sem("act_lo")
        sig_done = sem("sig_done")
        f_ready, lf_ready, d_ready, e_ready, qk_ready = (sem(s) for s in (
            "f_ready", "lf_ready", "d_ready", "e_ready", "qk_ready"))
        aT_done, aT_copied, aT_ready = sem("aT_done"), sem("aT_copied"), sem("aT_ready")
        kl_done, kl_ready = sem("kl_done"), sem("kl_ready")
        ds_done, state_ready = sem("ds_done"), sem("state_ready")
        o_done, o_copied, ss_ready, rms_ready, yb_ready, ybT_done = (sem(s) for s in (
            "o_done", "o_copied", "ss_ready", "rms_ready", "yb_ready", "ybT_done"))
        s_done, s_max, p_exp, p_ready, pT_done, pT_ready, pv_done, ya_copied = (sem(s) for s in (
            "s_done", "s_max", "p_exp", "p_ready", "pT_done", "pT_ready", "pv_done", "ya_copied"))
        gt1_done, gt2_done, mod2_done, gt1_ready, gt2_ready = (sem(s) for s in (
            "gt1_done", "gt2_done", "mod2_done", "gt1_ready", "gt2_ready"))
        gates_ready, mix_ready, m_hi_ready, m_lo_ready = (sem(s) for s in (
            "gates_ready", "mix_ready", "m_hi_ready", "m_lo_ready"))
        x_landed, keys_cleared, keys_landed = sem("x_landed"), sem("keys_cleared"), sem("keys_landed")
        var_ready, std_ready, x1_ready, x1T_done, h2f_ready = (sem(s) for s in (
            "var_ready", "std_ready", "x1_ready", "x1T_done", "h2f_ready"))
        xn_ready, h2f_act_ready, mod2_ln_ready = sem("xn_ready"), sem("h2f_act_ready"), sem("mod2_ln_ready")
        gt2_spilled, x1_spilled = sem("gt2_spilled"), sem("x1_spilled")
        out_done = sem("out_done")
        score_done, score_copied = sem("score_done"), sem("score_copied")
        u_taken = sem("u_taken")
        s_in_ready, s_in_used = sem("s_in_ready"), sem("s_in_used")
        best_ready, gate_exp, gate_ready = sem("best_ready"), sem("gate_exp"), sem("gate_ready")
        idxT_done = sem("idxT_done")
        ohi_ready, ohj_ready, ohj_act_ready, oh_used, g_lo_taken, g_hi_taken = (sem(s) for s in (
            "ohi_ready", "ohj_ready", "ohj_act_ready", "oh_used", "g_lo_taken", "g_hi_taken"))
        prod_ready = sem("prod_ready")
        wsplit_hi, wsplit_lo = sem("wsplit_hi"), sem("wsplit_lo")
        end_landed, y_done = sem("end_landed"), sem("y_done")
        var2_ready, std2_ready, zn_ready, z2_scaled = sem("var2_ready"), sem("std2_ready"), sem("zn_ready"), sem("z2_scaled")
        z2_ready = [sem(f"z2_ready{t}") for t in range(TT)]

        block = ctx.enter_context(nc.Block())

        def dest(n):
            return raw[:, n % S_RAW].rearrange("p h n -> p (h n)")

        def u_src(g):
            return u_d[bass.ds(g, 1)].rearrange("a p n -> p (a n)")

        def v_src(g):
            return v_d[bass.ds(g, 1)].rearrange("a p n -> p (a n)")

        @block.sync
        def _(sp):
            def raw_free(n):
                sp.wait_ge(hi_ready, 2 * n - 2)
                sp.wait_ge(lo_ready, 2 * n - 2)

            def load_block(n):
                if n >= S_RAW:
                    raw_free(n)
                sp.dma_start(dest(n), ws_d[n]).then_inc(raw_landed[n % S_RAW], 16)

            def load_ada(t):
                third, k, half = ada_tile(t)
                if t >= ADA_SLOTS:
                    sp.wait_ge(ada_done, t - ADA_SLOTS + 1)
                col = third * 2 * ADA_W + half * ADA_W
                sp.dma_start(ada[:, t % ADA_SLOTS], w_ada_d[k * P:(k + 1) * P, col:col + ADA_W]) \
                    .then_inc(ada_landed[t % ADA_SLOTS], 16)

            def load_bias(g):
                sp.wait_ge(acc_cleared, g + 1)
                sp.dma_start(acc[0:1, g % 2], b_ada_d[0:1, g * 2 * ADA_W:(g + 1) * 2 * ADA_W]) \
                    .then_inc(bias_landed[g], 16)

            sp.dma_start(c_col[:, :], c_d).then_inc(small_landed, 16)
            sp.dma_start(lb_raw[:, :], lb_d).then_inc(small_landed, 16)
            for t in range(2):
                load_ada(t)
            load_bias(0)
            for t in range(2, ADA_THIRD):
                load_ada(t)
            sp.dma_start(xT[:, :, :], xT_d.rearrange("(k p) t -> p k t", p=P)).then_inc(xT_landed, 16)
            load_block(0)
            load_block(1)
            load_bias(1)
            sp.dma_start(norm_g[:, :], norm_g_d.partition_broadcast(P)).then_inc(norm_landed, 16)
            for b in range(2, NA):
                load_block(b)
                for t in ada_at(b):
                    if t == 2 * ADA_THIRD:
                        load_bias(2)
                    load_ada(t)
                if b == BRANCH + 2:
                    sp.wait_ge(pv_done, HEADS)
                    sp.dma_start(x_nat[:, :, :], x_d.rearrange("(a p) n -> p a n", p=P)).then_inc(x_landed, 16)
                    sp.dma_start(ln1_g[:, :], ln1_g_d.partition_broadcast(P)).then_inc(x_landed, 16)
                    sp.dma_start(ln1_b[:, :], ln1_b_d.partition_broadcast(P)).then_inc(x_landed, 16)
                    sp.dma_start(ln_cols[:, :], ln1_cols_d).then_inc(x_landed, 16)
                if b == WQ:
                    sp.wait_ge(keys_cleared, 1)
                    for half in range(2):
                        q = slice(half * DH, (half + 1) * DH)
                        sp.dma_start(keys[q, :, half * NK:(half + 1) * NK], keys_d[q]).then_inc(keys_landed, 16)
            with sp.Fori(0, G1 // 2) as i:
                for e in range(2):
                    raw_free(2 * i + (U0 + e))
                    sp.dma_start(dest(U0 + e), u_src(2 * i + e)).then_inc(raw_landed[(U0 + e) % S_RAW], 16)
            raw_free(U0 + G1)
            sp.dma_start(dest(U0 + G1), u_src(G1)).then_inc(raw_landed[(U0 + G1) % S_RAW], 16)
            with sp.Fori(0, STEPS) as q:
                raw_free(2 * q + U2)
                sp.dma_start(dest(U2), u_src(q + (G1 + 1))).then_inc(raw_landed[U2 % S_RAW], 16)
                raw_free(2 * q + (U2 + 1))
                sp.dma_start(dest(U2 + 1), v_src(q + G1)).then_inc(raw_landed[(U2 + 1) % S_RAW], 16)
            raw_free(V2)
            sp.dma_start(dest(V2), v_src(NG - 1)).then_inc(raw_landed[V2 % S_RAW], 16)
            with sp.Fori(0, G1 // 2) as i:
                for e in range(2):
                    raw_free(2 * i + (V2 + 1 + e))
                    sp.dma_start(dest(V2 + 1 + e), v_src(2 * i + e)).then_inc(raw_landed[(V2 + 1 + e) % S_RAW], 16)
            for t in range(TT):
                sp.wait_ge(z2_ready[t], 1)
                sp.dma_start(out_d[t * P:(t + 1) * P, :], z2[:, t]).then_inc(out_done, 16)
            sp.wait_ge(out_done, 16 * TT)

        @block.gpsimd
        def _(pool):
            n = [0]

            def link(ins):
                n[0] += 1
                ins.then_inc(pool_chain, 1)
                pool.wait_ge(pool_chain, n[0])

            for g in range(2):
                nc.gpsimd.memset(acc[:, g], 0.0).then_inc(acc_cleared, 1)
            nc.gpsimd.memset(ones_pp[:, :], 1.0)
            nc.gpsimd.memset(ones_col[:, :], 1.0).then_inc(consts, 1)
            link(nc.gpsimd.memset(ident[:, :], 0.0))
            nc.gpsimd.affine_select(out=ident[:, :], in_=ident[:, :], compare_op=ALU.not_equal, fill=1.0,
                                    base=0, pattern=[[-1, P]], channel_multiplier=1).then_inc(consts, 1)
            link(nc.gpsimd.iota(dist[:, 0:P].bitcast(I32), pattern=[[-1, P]], base=0, channel_multiplier=1))
            link(nc.gpsimd.iota(dist[:, P:3 * P].bitcast(I32), pattern=[[-1, 2 * P]], base=P, channel_multiplier=1))
            link(nc.gpsimd.tensor_copy(dist[:, :], dist[:, :].bitcast(I32)))
            link(nc.gpsimd.affine_select(out=dist[:, 0:P], in_=dist[:, 0:P], compare_op=ALU.is_ge, fill=FAR,
                                         base=0, pattern=[[-1, P]], channel_multiplier=1))
            nc.gpsimd.affine_select(out=dist[:, P:3 * P], in_=dist[:, P:3 * P], compare_op=ALU.is_ge, fill=FAR,
                                    base=P, pattern=[[-1, 2 * P]], channel_multiplier=1).then_inc(consts, 1)
            link(nc.gpsimd.iota(iota[:, :].bitcast(I32), pattern=[[1, P]], base=0, channel_multiplier=0))
            nc.gpsimd.tensor_copy(iota[:, :], iota[:, :].bitcast(I32)).then_inc(consts, 1)
            link(nc.gpsimd.memset(scan_m[:, :], 1.0))
            nc.gpsimd.memset(scan_m[:, :].rearrange("p (n c) -> p n c", c=CH)[:, :, 0:1], 0.0).then_inc(consts, 1)
            nc.gpsimd.memset(aT[:, :, :, :], 0.0).then_inc(consts, 1)
            pool.wait_ge(mod1_ready, 1)
            nc.gpsimd.memset(acc[:, 0], 0.0).then_inc(acc_cleared, 1)
            for b in POOL_LO:
                m0 = (2 * b + 1) % S_PIECE
                pool.wait_ge(lo_ready, 2 * b + 1)
                pool.wait_ge(hi_ready, 2 * b + 2)
                nc.gpsimd.tensor_tensor(w_lo[:, m0], raw[:, b % S_RAW, 1], w_hi[:, m0].bitcast(F32), ALU.subtract) \
                    .then_inc(lo_ready, 1)
                if b == 16:
                    pool.wait_ge(aT_copied, TT)
                    nc.gpsimd.affine_select(out=aT[:, :, :, :].rearrange("p a h t -> p (a h) t"),
                                            in_=aT[:, :, :, :].rearrange("p a h t -> p (a h) t"),
                                            compare_op=ALU.is_ge, fill=0.0, base=0,
                                            pattern=[[0, TT * HG], [1, P]], channel_multiplier=-1).then_inc(aT_ready, 1)
            pool.wait_ge(mod2_done, 1)
            pool.wait_ge(gt1_done, 1)
            nc.gpsimd.memset(keys[:, :, :], 0.0).then_inc(keys_cleared, 1)
            pool.wait_ge(gt2_ready, 1)
            pool.dma_start(gt2_d, gt2_row[0:1, :]).then_inc(gt2_spilled, 16)
            pool.wait_ge(x1_ready, TT)
            pool.dma_start(x1_d.rearrange("(a p) n -> p a n", p=P), x1[:, :, :]).then_inc(x1_spilled, 16)
            pool.wait_ge(gt2_spilled, 16)
            pool.wait_ge(x1_spilled, 16)
            pool.wait_ge(lo_ready, 2 * U0 + 2)
            with pool.Fori(0, G1 // 2) as i:
                for n0 in (U0 + 1, U0 + 2):
                    for e in range(2):
                        m0 = (2 * n0 + e) % S_PIECE
                        pool.wait_ge(hi_ready, 4 * i + (2 * n0 + e + 1))
                        nc.gpsimd.nop(nofuse=True)
                        nc.gpsimd.tensor_tensor(w_lo[:, m0], raw[:, n0 % S_RAW, e], w_hi[:, m0].bitcast(F32), ALU.subtract) \
                            .then_inc(lo_ready, 1)
            pool.wait_ge(g_hi_taken, S_OH)
            start = n[0]
            with pool.Fori(0, GROUPS // S_OH) as i:
                for e in range(S_OH):
                    pool.wait_ge(oh_used, S_OH * i + (e + 1))
                    nc.gpsimd.tensor_copy(j_col[:, 2 * e:2 * e + 2], idx[:, 1, bass.ds(4 * S_OH * i + (4 * e + 2), 2)]).then_inc(pool_chain, 1)
                    pool.wait_ge(pool_chain, S_OH * i + (start + e + 1))
                    nc.gpsimd.nop(nofuse=True)
                    for y in range(2):
                        last = nc.gpsimd.tensor_scalar(oh_j[e][:, 2 + y], iota[:, :], j_col[:, 2 * e + y:2 * e + y + 1], None,
                                                       ALU.is_equal)
                    last.then_inc(ohj_ready, 1)
            pool.wait_ge(piece_used, 2 * V2 + 2)
            pool.dma_start(x1_b[:, :, :], x1_d.rearrange("(a p) n -> p a n", p=P)).then_inc(end_landed, 16)
            pool.dma_start(gt2_b[:, :], gt2_d.rearrange("a n -> (a n)").partition_broadcast(P)).then_inc(end_landed, 16)
            pool.dma_start(ln2_g[:, :], ln2_g_d.partition_broadcast(P)).then_inc(end_landed, 16)
            pool.dma_start(ln2_b[:, :], ln2_b_d.partition_broadcast(P)).then_inc(end_landed, 16)
            pool.wait_ge(end_landed, 64)
            pool.wait_ge(zn_ready, 1)
            nc.gpsimd.tensor_tensor(z2[:, 0], z2[:, 0], ln2_g[:, :], ALU.mult).then_inc(z2_scaled, 1)
            pool.wait_ge(z2_scaled, 1)
            nc.gpsimd.tensor_tensor(z2[:, 0], z2[:, 0], ln2_b[:, :], ALU.add).then_inc(z2_ready[0], 1)

        @block.scalar
        def _(act):
            def copy(out, in_, **kw):
                return nc.scalar.activation(out, in_, ACT.Copy, **kw)

            def split_hi(n, landed, slot_block):
                s = slot_block % S_RAW
                act.wait_ge(raw_landed[s], landed)
                for e in range(2):
                    m = 2 * n + e
                    if not isinstance(m, int) or m >= S_PIECE:
                        act.wait_ge(piece_used, m - S_PIECE + 1)
                    copy(w_hi[:, (2 * slot_block + e) % S_PIECE], raw[:, s, e]).then_inc(hi_ready, 1)

            act.wait_ge(lb_max_ready, 1)
            nc.scalar.activation(lb_e[:, :], lb_e[:, :], ACT.Exp).then_inc(lb_e_ready, 1)
            act.wait_ge(small_landed, 32)
            nc.scalar.activation(c_sig[:, :], c_col[:, :], ACT.Sigmoid).then_inc(c_sig_ready, 1)

            for b in range(NA):
                split_hi(b, 16 * (b // S_RAW + 1), b)
                if b == 0:
                    for half in range(2):
                        q = slice(half * KC // 2, (half + 1) * KC // 2)
                        act.wait_ge(h_ready, half + 1)
                        copy(a_hi[:, q], xT[:, q]).then_inc(act_hi, 1)
                e = b - 2
                if e >= 0:
                    s = e % 2
                    act.wait_ge(piece_used, 2 * e + 2)
                if HF <= e < HF + 2:
                    r = e - HF
                    nc.scalar.activation(lf[:, r * 512:(r + 1) * 512], pw[s][:, :], ACT.Sigmoid).then_inc(act_took, 1)
                if HQ <= e < HQ + 2:
                    r = e - HQ
                    nc.scalar.activation(qh[:, r * 512:(r + 1) * 512], pw[s][:, :], ACT.Sigmoid).then_inc(sig_done, 1)
                if HI <= e < HI + 2 or VA <= e < VA + 2:
                    dst, r = (vh, e - HI) if e < VA else (va, e - VA)
                    copy(dst[:, 0, r * 256:(r + 1) * 256], pw[s][:, 0:256])
                    copy(dst[:, 1, r * 256:(r + 1) * 256], pv[s][:, 0:256]).then_inc(act_took, 1)
                if HGATE <= e < HGATE + 2:
                    r = e - HGATE
                    for t, src in enumerate((pw[s], pv[s])):
                        last = nc.scalar.activation(sgh[:, t, r * 256:(r + 1) * 256], src[:, 0:256], ACT.Sigmoid)
                    last.then_inc(sig_done, 1)
                for lo, dst, scale in ((QA, qT, DH ** -0.5), (KA, kT, 1.0)):
                    if lo <= e < lo + 2:
                        r = e - lo
                        copy(dst[:, 2 * r:2 * r + 2], pw[s][:, :].rearrange("p (c t) -> p c t", c=2), scale=scale) \
                            .then_inc(act_took, 1)
                for lo, dst in ((GA, sig_a), (GB, sig_b)):
                    if lo <= e < lo + 4:
                        r = e - lo
                        copy(dst[:, 2 * r:2 * r + 2], pw[s][:, :].rearrange("p (c t) -> p c t", c=2)).then_inc(act_took, 1)
                if b == 10:
                    act.wait_ge(f_ready, 1)
                    nc.scalar.activation(lf[:, :], lf[:, :], ACT.Ln).then_inc(lf_ready, 1)
                if b == 11:
                    act.wait_ge(d_ready, 2)
                    nc.scalar.activation(k_e[:, :], q_e[:, :], ACT.Exp, scale=-1.0).then_inc(act_chain, 1)
                    act.wait_ge(act_chain, 1)
                    nc.scalar.activation(q_e[:, :], q_e[:, :], ACT.Exp)
                    nc.scalar.activation(k_l[:, :], k_l[:, :], ACT.Exp)
                    nc.scalar.activation(q_x[:, :], bcum[:, :], ACT.Exp)
                    nc.scalar.activation(decay[:, :], bcum[:, :].rearrange("p (n c) -> p n c", c=CH)[:, :, CH - 1],
                                         ACT.Exp).then_inc(e_ready, 1)
                if b == 16:
                    for t, src in enumerate((px[3], pv[0])):
                        act.wait_ge(aT_done, t + 1)
                        if t == 0:
                            act.wait_ge(consts, 6)
                        for c in range(2):
                            q = slice(c * CH, (c + 1) * CH)
                            last = copy(aT[q, t, :, c * CH:(c + 1) * CH],
                                        src[q, :].rearrange("p (h t) -> p h t", h=HG)[:, :, c * CH:(c + 1) * CH])
                        last.then_inc(aT_copied, 1)
                if b == 17:
                    for t, src in enumerate((pv[1], px[3])):
                        act.wait_ge(kl_done, t + 1)
                        copy(kl_nat[:, t], src[:, :].rearrange("p (h t) -> p h t", h=HG)).then_inc(kl_ready, 1)
                if b == 21:
                    for t, src in enumerate((px[3], pv[0])):
                        act.wait_ge(o_done, t + 1)
                        copy(o_nat[:, t], src[:, :]).then_inc(o_copied, 1)
                h = b - 15
                if 0 <= h < HEADS:
                    act.wait_ge(s_max, h + 1)
                    x = h % 2
                    for t, q in enumerate((slice(0, P), slice(P, 3 * P))):
                        last = nc.scalar.activation(prob[:, x, q], prob[:, x, q], ACT.Exp,
                                                    bias=rmax[:, 2 * x + t:2 * x + t + 1],
                                                    accum_out=rsum[:, 2 * x + t:2 * x + t + 1])
                    last.then_inc(p_exp, 1)
                h = b - 16
                if 0 <= h < HEADS:
                    act.wait_ge(pT_done, h + 1)
                    if h >= 1:
                        act.wait_ge(pv_done, h)
                    copy(pT[:, :], px[1][:, 0:3 * P]).then_inc(pT_ready, 1)
                if b == 21:
                    act.wait_ge(ss_ready, 1)
                    nc.scalar.activation(rms[:, :], sumsq[:, :], ACT.Sqrt).then_inc(rms_ready, 1)
                for h in range(1, HEADS, 2):
                    if b == min(h + 17, 23):
                        act.wait_ge(pv_done, h + 1)
                        copy(yaT[:, h // 2], px[2][:, 0:T]).then_inc(ya_copied, 1)
                if b == 23:
                    act.wait_ge(ya_copied, HEADS // 2)
                    copy(a_hi[:, 0:4], yaT[:, :, :]).then_inc(act_hi, 1)
                    for t, src in enumerate((pv[1], px[3])):
                        act.wait_ge(ybT_done, t + 1)
                        last = copy(a_hi[:, 4:8, t * P:(t + 1) * P], src[:, :].rearrange("p (h t) -> p h t", h=HG))
                    last.then_inc(act_hi, 1)
                    for dst in (sig_a, sig_b):
                        act.wait_ge(act_took, evac_count(GB + 3))
                        last = nc.scalar.activation(dst[:, :, :], dst[:, :, :], ACT.Sigmoid)
                    last.then_inc(gates_ready, 1)
                if BRANCH <= e < BRANCH + 4:
                    r = e - BRANCH
                    act.wait_ge(mix_ready, r + 1)
                    copy(m_hi[:, 2 * r:2 * r + 2], mix[:, :].rearrange("p (c t) -> p c t", c=2)).then_inc(m_hi_ready, 1)
                if e == WOUT + 1:
                    act.wait_ge(consts, 1)
                    nc.scalar.activation(warm[:, :], ones_col[:, :], ACT.Sqrt)
                if e == WOUT + 3:
                    act.wait_ge(var_ready, 1)
                    nc.scalar.activation(std[:, :], std[:, :], ACT.Sqrt).then_inc(std_ready, 1)
                    act.wait_ge(mod2_ln_ready, 1)
                    act.wait_ge(x1T_done, 1)
                    for k in range(KC // 2, KC):
                        last = nc.scalar.activation(h2f[:, k], px[k // 2][:, (k % 2) * T:(k % 2 + 1) * T], ACT.Identity,
                                                    scale=mod2[:, KC + k:KC + k + 1], bias=mod2[:, k:k + 1])
                    last.then_inc(h2f_act_ready, 1)
                    for half, s_h2f in enumerate((h2f_ready, h2f_act_ready)):
                        q = slice(half * KC // 2, (half + 1) * KC // 2)
                        act.wait_ge(s_h2f, 1)
                        copy(a_hi[:, q], h2f[:, q]).then_inc(act_hi, 1)
                if WQ <= e:
                    r = e - WQ
                    copy(qpT[:, 2 * r:2 * r + 2], pw[s][:, :].rearrange("p (c t) -> p c t", c=2)).then_inc(act_took, 1)

            split_hi(U0, 16 * (U0 // S_RAW + 1), U0)
            for e in range(NA - 2, NA):
                act.wait_ge(piece_used, 2 * e + 2)
                r = e - WQ
                copy(qpT[:, 2 * r:2 * r + 2], pw[e % 2][:, :].rearrange("p (c t) -> p c t", c=2)).then_inc(u_taken, 1)
            for c in range(PH // 2):
                for t in range(TT):
                    act.wait_ge(score_done, 2 * c + t + 1)
                    copy(score[:, t * PH + 2 * c:t * PH + 2 * c + 2],
                         px[(2 * c + t) % 4][:, :].rearrange("p (h n) -> p h n", h=2)).then_inc(score_copied, 1)
            act.wait_ge(score_copied, PH)
            act.wait_ge(gt2_spilled, 16)
            act.wait_ge(x1_spilled, 16)
            def load_scores(i):
                copy(s_in[:, :, :].rearrange("p a n -> p (a n)"),
                     score[:, bass.ds(i, 1)].rearrange("p a n -> p (a n)")).then_inc(s_in_ready, 1)

            def gelu_pair(i, e):
                act.wait_ge(piece_used, 4 * i + (2 * (U0 + e) + 2))
                nc.scalar.activation(W[:, bass.ds(4 * i + 2 * e, 2)],
                                     pw[e][:, :].rearrange("p (j t) -> p j t", j=2), ACT.Gelu).then_inc(u_taken, 1)

            load_scores(0)
            for n0 in (U0 + 1, U0 + 2):
                split_hi(n0, 16 * (n0 // S_RAW + 1), n0)
            with act.Fori(0, G1 // 2 - 1) as i:
                for e in range(2):
                    gelu_pair(i, e)
                    n0 = U0 + e + 3
                    split_hi(2 * i + n0, 16 * i + 16 * (n0 // S_RAW + 1), n0)
                    if e == 0:
                        act.wait_ge(s_in_used, i + 1)
                        load_scores(i + 1)
            for e in range(2):
                gelu_pair(G1 // 2 - 1, e)
            act.wait_ge(best_ready, 1)
            nc.scalar.activation(gate[:, :, :], gate[:, :, :], ACT.Exp).then_inc(gate_exp, 1)
            for a in range(2):
                act.wait_ge(idxT_done, 1)
                copy(idx[:, a], px[2][:, a * T:(a + 1) * T]).then_inc(g_hi_taken, S_OH // 2)
            act.wait_ge(g_hi_taken, S_OH)

            def one_hot_j(i, e):
                k = e % S_OH
                act.wait_ge(oh_used, S_OH * i + (e + 1))
                for y in range(2):
                    last = nc.scalar.activation(oh_j[k][:, y], iota[:, :], ACT.Abs, scale=-1.0,
                                                bias=idx[:, 1, bass.ds(4 * S_OH * i + (4 * e + y), 1)])
                last.then_inc(act_chain, 1)
                act.wait_ge(act_chain, S_OH * i + (e + 2))
                nc.scalar.activation(oh_j[k][:, 0:2], oh_j[k][:, 0:2], ACT.Relu, scale=-1.0, bias=ones_col[:, :]) \
                    .then_inc(ohj_act_ready, 1)

            def take_upper(i, e):
                act.wait_ge(oh_used, S_OH * i + (S_OH + e + 1))
                copy(W[:, 2 * G1:NK, bass.ds(4 * S_OH * i + 4 * e, 4)],
                     pg[e][:, :].rearrange("p (t j) -> p j t", t=4)[:, 2 * G1:NK]).then_inc(g_hi_taken, 1)

            for e in range(2):
                one_hot_j(0, e)
            with act.Fori(0, GROUPS // S_OH - 1) as i:
                for e in range(S_OH):
                    one_hot_j(i, e + 2)
                    take_upper(i, e)
            for e in range(S_OH):
                if e + 2 < S_OH:
                    one_hot_j(GROUPS // S_OH - 1, e + 2)
                take_upper(GROUPS // S_OH - 1, e)

            def gelu(q):
                nc.scalar.activation(gel[:, :], pw[0][:, :], ACT.Gelu).then_inc(u_taken, 1)

            def split_w(q, pair, used, e):
                act.wait_ge(piece_used, used + e)
                copy(ws_hi[:, e], W[:, bass.ds(2 * pair + e, 1)].rearrange("p a t -> p (a t)")).then_inc(wsplit_hi, 1)

            act.wait_ge(piece_used, 2 * (U0 + G1) + 2)
            act.wait_ge(oh_used, GROUPS + S_OH)
            gelu(0)
            with act.Fori(0, STEPS) as q:
                split_hi(2 * q + U2, 16 * q + 16 * (U2 // S_RAW + 1), U2)
                act.wait_ge(prod_ready, q + 1)
                for e in range(2):
                    split_w(q, q + G1, 4 * q + (2 * U2 - 1), e)
                split_hi(2 * q + (U2 + 1), 16 * q + 16 * ((U2 + 1) // S_RAW + 1), U2 + 1)
                act.wait_ge(piece_used, 4 * q + (2 * U2 + 2))
                gelu(q + 1)
            split_hi(V2, 16 * (V2 // S_RAW + 1), V2)
            act.wait_ge(prod_ready, STEPS + 1)
            for e in range(2):
                split_w(STEPS, NG - 1, 2 * V2 - 1, e)
            with act.Fori(0, G1 // 2) as i:
                for x in range(2):
                    n0 = V2 + 1 + x
                    split_hi(2 * i + n0, 16 * i + 16 * (n0 // S_RAW + 1), n0)
                    for e in range(2):
                        split_w(0, 2 * i + x, 4 * i + (2 * n0 - 1), e)
            nc.scalar.activation(warm[:, :], ones_col[:, :], ACT.Sqrt)
            for t in range(TT):
                act.wait_ge(var2_ready, t + 1)
                nc.scalar.activation(std[:, t:t + 1], std[:, t:t + 1], ACT.Sqrt).then_inc(std2_ready, 1)

        @block.tensor
        def _(pe):
            def three(out, pairs, start=True, stop=True):
                for x, (lh, ll, rh, rl) in enumerate(pairs):
                    nc.tensor.matmul(out, lh, rh, start=start and x == 0, stop=False)
                    nc.tensor.matmul(out, lh, rl, start=False, stop=False)
                    last = nc.tensor.matmul(out, ll, rh, start=False, stop=stop and x == len(pairs) - 1)
                return last

            def weights(m):
                s = m % S_PIECE
                return w_hi[:, s], w_lo[:, s]

            def columns_piece(m, out, act_chunk=0, chunks=KC, cols=P, halves=None):
                hi, lo = (w.rearrange("p (k c) -> p k c", k=chunks) for w in weights(m))
                if halves is not None:
                    for half in range(2):
                        pe.wait_ge(act_lo, halves + half + 1)
                        last = three(out, [(hi[:, k], lo[:, k], a_hi[:, k], a_lo[:, k])
                                           for k in range(half * KC // 2, (half + 1) * KC // 2)], start=half == 0, stop=half == 1)
                    last.then_inc(piece_used, 1)
                    return
                for c in range(cols // P):
                    q = slice(c * P, (c + 1) * P)
                    last = three(out[:, c * T:(c + 1) * T],
                                 [(hi[:, k, q], lo[:, k, q], a_hi[:, act_chunk + k], a_lo[:, act_chunk + k])
                                  for k in range(chunks)])
                last.then_inc(piece_used, 1)

            def rows_piece(b, h, x_hi, x_lo):
                hi, lo = (w.rearrange("p (k c) -> p k c", k=KC // 2) for w in weights(2 * b + h))
                for t, bk in enumerate((pw[b % 2], pv[b % 2])):
                    q = slice(t * P, (t + 1) * P)
                    last = three(bk[:, 0:256],
                                 [(x_hi[:, 4 * h + k, q], x_lo[:, 4 * h + k, q], hi[:, k], lo[:, k])
                                  for k in range(KC // 2)], start=h == 0, stop=h == 1)
                last.then_inc(piece_used, 1)

            pe.wait_ge(consts, 1)
            for c in range(2 * KC):
                if c % KC == 0:
                    pe.wait_ge(ada_done, c + KC)
                last = nc.tensor.matmul(px[0][:, c:c + 1], acc[:, 0, c * P:(c + 1) * P], ones_col[:, :],
                                        start=True, stop=True)
            last.then_inc(mod1_ready, 1)

            def after(b):
                if b == 14:
                    pe.wait_ge(qk_ready, 2)
                    pe.wait_ge(act_took, evac_count(12))
                    for t, dst in enumerate((px[3], pv[0])):
                        for h in range(HG):
                            q = slice(h * T + t * P, h * T + (t + 1) * P)
                            last = nc.tensor.matmul(dst[:, h * P:(h + 1) * P], k_e[:, q], q_e[:, q], start=True, stop=True)
                        last.then_inc(aT_done, 1)
                if b == 15:
                    pe.wait_ge(act_took, evac_count(13))
                    for t, dst in enumerate((pv[1], px[3])):
                        if t:
                            pe.wait_ge(aT_copied, 1)
                        for h in range(HG):
                            q = slice(h * T + t * P, h * T + (t + 1) * P)
                            last = nc.tensor.transpose(dst[:, h * P:(h + 1) * P], k_l[:, q], ident[:, :])
                        last.then_inc(kl_done, 1)
                if b in (16, 17):
                    for n in ((0,) if b == 16 else (1, 2)):
                        dst = (pv[0], pv[1], px[3])[n]
                        pe.wait_ge(kl_ready, n // 2 + 1)
                        pe.wait_ge(aT_copied, 2)
                        if n:
                            pe.wait_ge(kl_ready, 2)
                        t, q = n // 2, slice((n % 2) * CH, (n % 2 + 1) * CH)
                        for h in range(HG):
                            last = nc.tensor.matmul(dst[:, h * P:(h + 1) * P], kl_nat[q, t, h],
                                                    vh[q, t, h * P:(h + 1) * P], start=True, stop=True)
                        last.then_inc(ds_done, 1)
                if b == 19:
                    pe.wait_ge(aT_ready, 1)
                    pe.wait_ge(state_ready, 3)
                    for t, dst in enumerate((px[3], pv[0])):
                        for h in range(HG):
                            o = slice(h * P, (h + 1) * P)
                            for c in range(2):
                                n, r = 2 * t + c, slice(c * CH, (c + 1) * CH)
                                last = nc.tensor.matmul(dst[r, o], aT[:, t, h, r], vh[:, t, o], start=True, stop=n == 0)
                                if n:
                                    x = h * T + n * CH
                                    last = nc.tensor.matmul(dst[r, o], q_x[:, x:x + CH], state[:, n - 1, o],
                                                            start=False, stop=True)
                        last.then_inc(o_done, 1)
                h = b - 13
                if 0 <= h < HEADS:
                    pe.wait_ge(act_took, evac_count(KA + 1))
                    if h >= 1:
                        pe.wait_ge(s_max, h)
                    r = slice((h % 2) * DH, (h % 2 + 1) * DH)
                    nc.tensor.matmul(px[0][:, 0:P], qT[r, h // 2, 0:P], kT[r, h // 2, 0:P], start=True, stop=True)
                    nc.tensor.matmul(px[0][:, P:3 * P], qT[r, h // 2, P:T], kT[r, h // 2, :], start=True, stop=True) \
                        .then_inc(s_done, 1)

                def transposes(h):
                    pe.wait_ge(p_ready, h + 1)
                    if h >= 1:
                        pe.wait_ge(pT_ready, h)
                    for x in range(3):
                        last = nc.tensor.transpose(px[1][:, x * P:(x + 1) * P], prob[:, h % 2, x * P:(x + 1) * P], ident[:, :])
                    last.then_inc(pT_done, 1)

                def values(h):
                    pe.wait_ge(pT_ready, h + 1)
                    pe.wait_ge(act_took, evac_count(VA + 1))
                    if h >= 2 and h % 2 == 0:
                        pe.wait_ge(ya_copied, h // 2)
                    o, v = slice((h % 2) * DH, (h % 2 + 1) * DH), slice(h * DH, (h + 1) * DH)
                    nc.tensor.matmul(px[2][o, 0:T], va[:, 0, v], pT[:, 0:T], start=True, stop=False)
                    nc.tensor.matmul(px[2][o, P:T], va[:, 1, v], pT[:, T:3 * P], start=False, stop=True).then_inc(pv_done, 1)

                if 0 <= b - 14 < HEADS:
                    transposes(b - 14)
                if 0 <= b - 15 < HEADS - 1:
                    values(b - 15)
                if b == 21:
                    pe.wait_ge(yb_ready, 1)
                    for t, dst in enumerate((pv[1], px[3])):
                        for c in range(HG):
                            last = nc.tensor.transpose(dst[:, c * P:(c + 1) * P], o_nat[:, t, c * P:(c + 1) * P], ident[:, :])
                        last.then_inc(ybT_done, 1)
                    values(HEADS - 1)
                if b == WOUT - 1:
                    pe.wait_ge(ada_done, ADA_TILES)
                    pe.wait_ge(pT_ready, HEADS)
                    for half in range(2):
                        last = nc.tensor.matmul(px[half][:, :], ones_pp[:, :], acc[:, 1, half * 512:(half + 1) * 512],
                                                start=True, stop=True)
                    last.then_inc(gt1_done, 1)
                if b == WOUT:
                    pe.wait_ge(ya_copied, HEADS // 2)
                    for c in range(KC):
                        nc.tensor.matmul(px[2][:, c:c + 1], acc[:, 1, ADA_W + c * P:ADA_W + (c + 1) * P],
                                         ones_col[:, :], start=True, stop=True)
                    for c in range(KC):
                        last = nc.tensor.matmul(px[2][:, KC + c:KC + c + 1], acc[:, 0, c * P:(c + 1) * P],
                                                ones_col[:, :], start=True, stop=True)
                    last.then_inc(mod2_done, 1)
                if b == WOUT + 1:
                    pe.wait_ge(gt1_ready, 1)
                    for half in range(2):
                        last = nc.tensor.matmul(px[half][0:1, :], ones_col[:, :],
                                                acc[:, 0, ADA_W + half * 512:ADA_W + (half + 1) * 512], start=True, stop=True)
                    last.then_inc(gt2_done, 1)

            for b in range(NA):
                for h in range(2):
                    m = 2 * b + h
                    pe.wait_ge(lo_ready, m + 1)
                    if h == 0 and b >= 2:
                        pe.wait_ge(dve_took if b - 2 in DVE_EVAC else act_took, evac_count(b - 2))
                    if b < BRANCH and b not in NATURAL:
                        columns_piece(m, pw[b % 2][:, h * T:(h + 1) * T], halves=0 if m == 0 else None)
                    elif b in NATURAL:
                        if b == WOUT:
                            pe.wait_ge(m_lo_ready, 2 * h + 2)
                        x_hi, x_lo = (a_hi, a_lo) if b < BRANCH else (m_hi, m_lo)
                        rows_piece(b, h, x_hi, x_lo)
                    elif b < WOUT:
                        if b == BRANCH and h == 0:
                            pe.wait_ge(act_lo, 4)
                        if b < BRANCH + 2 and h == 1:
                            pe.wait_ge(act_hi, 4)
                        columns_piece(m, (pw, pv)[h][b % 2], act_chunk=HG * h, chunks=HG, cols=2 * P)
                    else:
                        if b == WQ and h == 0:
                            for t in range(TT):
                                pe.wait_ge(xn_ready, t + 1)
                                for k in range(KC):
                                    at = (k % 2) * T + t * P
                                    last = nc.tensor.transpose(px[k // 2][:, at:at + P], x1[:, t, k * P:(k + 1) * P], ident[:, :])
                            last.then_inc(x1T_done, 1)
                        columns_piece(m, pw[b % 2][:, h * T:(h + 1) * T], halves=4 if m == 2 * WQ else None)
                after(b)

            pe.wait_ge(keys_landed, 32)
            for c in range(PH // 2):
                if c < 2:
                    pe.wait_ge(act_took, evac_count(WQ + c))
                else:
                    pe.wait_ge(u_taken, c - 1)
                for t in range(TT):
                    x = 2 * c + t
                    if x >= 4:
                        pe.wait_ge(score_copied, x - 3)
                    for h in range(2):
                        last = nc.tensor.matmul(px[x % 4][:, h * T:(h + 1) * T], qpT[:, 2 * c + h, t * P:(t + 1) * P],
                                                keys[:, 2 * c + h], start=True, stop=True)
                    last.then_inc(score_done, 1)

            def u_pair(n, n0, bk):
                for e in range(2):
                    pe.wait_ge(lo_ready, 2 * n + (e + 1))
                    columns_piece(2 * n0 + e, bk[:, e * T:(e + 1) * T])

            def v_part(n0, e, t, start, stop):
                hi, lo = weights(2 * n0 + e)
                q = slice(t * P, (t + 1) * P)
                for x, (l, r) in enumerate(((ws_hi, hi), (ws_hi, lo), (ws_lo, hi))):
                    for half in range(2):
                        last = nc.tensor.matmul(px[2 * t + half][:, :], l[:, e, q], r[:, half * 512:(half + 1) * 512],
                                                start=start and x == 0, stop=stop and x == 2)
                return last

            def v_pair(n, n0, split, first=False):
                for e in range(2):
                    pe.wait_ge(lo_ready, 2 * n + (e + 1))
                    pe.wait_ge(wsplit_lo, split + (e + 1))
                    for t in range(TT):
                        last = v_part(n0, e, t, start=first and e == 0, stop=False)
                    last.then_inc(piece_used, 1)

            with pe.Fori(0, G1 // 2) as i:
                for e in range(2):
                    pe.wait_ge(u_taken, 2 * i + (e + 1))
                    u_pair(2 * i + (U0 + e), U0 + e, pw[e])
            pe.wait_ge(u_taken, G1 + 1)
            u_pair(U0 + G1, U0 + G1, pw[0])
            pe.wait_ge(gate_ready, 1)
            for a, src in enumerate((ij[:, 0], ij[:, 1], gate[:, :, :])):
                for t in range(TT):
                    at = (a % 2) * T + t * P
                    last = nc.tensor.transpose(px[2 + a // 2][:, at:at + P],
                                               src[:, t * PH:(t + 1) * PH].rearrange("p h k -> p (h k)"), ident[:, :])
                last.then_inc(oh_used if a == 0 else idxT_done, S_OH if a == 0 else 1)
            with pe.Fori(0, GROUPS // S_OH) as i:
                for e in range(S_OH):
                    pe.wait_ge(g_lo_taken, S_OH * i + (e + 1))
                    pe.wait_ge(g_hi_taken, S_OH * i + (e + 1))
                    pe.wait_ge(ohi_ready, S_OH * i + (e + 1))
                    pe.wait_ge(ohj_ready, S_OH * i + (e + 1))
                    pe.wait_ge(ohj_act_ready, S_OH * i + (e + 1))
                    for tk in range(4):
                        last = nc.tensor.matmul(pg[e][:, tk * P:(tk + 1) * P], oh_i[e][:, tk], oh_j[e][:, tk],
                                                start=True, stop=True)
                    last.then_inc(oh_used, 1)
            def step(q, first=False):
                pe.wait_ge(u_taken, q + (G1 + 3))
                u_pair(2 * q + U2, U2, pw[0])
                v_pair(2 * q + (U2 + 1), U2 + 1, 2 * q, first=first)

            step(0, first=True)
            with pe.Fori(1, STEPS) as q:
                step(q)
            v_pair(V2, V2, 2 * STEPS)
            with pe.Fori(0, G1 // 2 - 1) as i:
                for x in range(2):
                    v_pair(2 * i + (V2 + 1 + x), V2 + 1 + x, 4 * i + (2 * (STEPS + 1 + x)))
            n = V2 + G1 - 1
            v_pair(n, n, 2 * (STEPS + G1 - 1))
            n = V2 + G1
            for t in range(TT):
                for e in range(2):
                    if t == 0:
                        pe.wait_ge(lo_ready, 2 * n + (e + 1))
                        pe.wait_ge(wsplit_lo, 2 * (STEPS + G1) + (e + 1))
                    last = v_part(n, e, t, start=False, stop=e == 1)
                last.then_inc(y_done, 1)

        @block.vector
        def _(dve):
            v = nc.vector

            chain = {"n": 0, "at": None}

            def link(ins):
                chain["n"] += 1
                ins.then_inc(dve_chain, 1)
                dve.wait_ge(dve_chain, chain["n"] if chain["at"] is None else chain["at"] + chain["n"])

            def mark(ins, s, value):
                ins.then_inc(s, 1)
                dve.wait_ge(s, value)

            def split_lo_piece(n, n0, e):
                m0 = (2 * n0 + e) % S_PIECE
                dve.wait_ge(hi_ready, 2 * n + (e + 1))
                v.tensor_tensor(w_lo[:, m0], raw[:, n0 % S_RAW, e], w_hi[:, m0].bitcast(F32), ALU.subtract).then_inc(lo_ready, 1)

            def split_lo(n, n0):
                for e in range(2):
                    split_lo_piece(n, n0, e)

            def sum_ada(t):
                third, k, half = ada_tile(t)
                if t % ADA_THIRD == 0:
                    dve.wait_ge(bias_landed[third], 16)
                dve.wait_ge(ada_landed[t % ADA_SLOTS], 16 * (t // ADA_SLOTS + 1))
                back = 1 if third == 0 else 2
                if t >= back:
                    dve.wait_ge(ada_done, t - back + 1)
                a = acc[:, third % 2, half * ADA_W:(half + 1) * ADA_W]
                v.scalar_tensor_tensor(a, ada[:, t % ADA_SLOTS], sc_col[:, k:k + 1], a, ALU.mult, ALU.add).then_inc(ada_done, 1)

            dve.wait_ge(small_landed, 32)
            link(v.tensor_tensor(lb_max[:, :], lb_raw[:, 0:HG], lb_raw[:, HG:2 * HG], ALU.max))
            mark(v.tensor_tensor(lb_e[:, :].rearrange("p (a h) -> p a h", a=2), lb_raw[:, :].rearrange("p (a h) -> p a h", a=2),
                                 lb_max[:, :].unsqueeze(1).broadcast_to([P, 2, HG]), ALU.subtract), lb_max_ready, 1)
            dve.wait_ge(lb_e_ready, 1)
            link(v.tensor_tensor(lb_max[:, :], lb_e[:, 0:HG], lb_e[:, HG:2 * HG], ALU.add))
            link(v.reciprocal(lb_max[:, :], lb_max[:, :]))
            link(v.tensor_tensor(lb_col[:, :], lb_e[:, 0:HG], lb_max[:, :], ALU.mult))
            link(v.tensor_scalar(om_lb[:, :], lb_col[:, :], -1.0, 1.0, ALU.mult, ALU.add))
            dve.wait_ge(c_sig_ready, 1)
            link(v.tensor_tensor(sc_col[:, :], c_col[:, :], c_sig[:, :], ALU.mult))
            for t in range(ADA_THIRD):
                sum_ada(t)
            dve.wait_ge(mod1_ready, 1)
            v.tensor_copy(mod1[:, 0:KC], px[0][:, 0:KC])
            link(v.tensor_scalar(mod1[:, KC:2 * KC], px[0][:, KC:2 * KC], 1.0, None, ALU.add))
            dve.wait_ge(xT_landed, 16)
            for k in range(KC):
                ins = v.tensor_scalar(xT[:, k], xT[:, k], mod1[:, KC + k:KC + k + 1], mod1[:, k:k + 1], ALU.mult, ALU.add)
                if k % 4 == 3:
                    mark(ins, h_ready, k // 4 + 1)

            def act_split_lo(src, stage):
                for half in range(2):
                    q = slice(half * KC // 2, (half + 1) * KC // 2)
                    dve.wait_ge(act_hi, stage + half + 1)
                    v.tensor_tensor(a_lo[:, q], src[:, q], a_hi[:, q].bitcast(F32), ALU.subtract).then_inc(act_lo, 1)

            for b in range(NA):
                h = b - 15
                if 0 <= h < HEADS:
                    x = h % 2
                    dve.wait_ge(s_done, h + 1)
                    if h == 0:
                        dve.wait_ge(consts, 3)
                    if h >= 2:
                        dve.wait_ge(pT_done, h - 1)
                    link(v.scalar_tensor_tensor(prob[:, x], dist[:, :], -(2.0 ** (-8.0 * (h + 1) / HEADS)), px[0][:, 0:3 * P],
                                                ALU.mult, ALU.add))
                    v.reduce_max(rmax[:, 2 * x:2 * x + 1], prob[:, x, 0:P], AX)
                    link(v.reduce_max(rmax[:, 2 * x + 1:2 * x + 2], prob[:, x, P:3 * P], AX))
                    mark(v.tensor_scalar(rmax[:, 2 * x:2 * x + 2], rmax[:, 2 * x:2 * x + 2], -1.0, None, ALU.mult), s_max, h + 1)
                if b >= 2:
                    if b - 1 in POOL_LO:
                        dve.wait_ge(lo_ready, 2 * b)
                    split_lo_piece(b, b, 0)
                    if b not in POOL_LO and not BRANCH <= b - 2 < BRANCH + 4:
                        split_lo_piece(b, b, 1)
                if b < 2:
                    split_lo(b, b)
                if b == 0:
                    act_split_lo(xT, 0)
                e = b - 2
                s = e % 2
                if HQ <= e < HQ + 2:
                    r = slice((e - HQ) * 512, (e - HQ + 1) * 512)
                    dve.wait_ge(sig_done, e - HQ + 1)
                    v.tensor_tensor(qh[:, r], pw[s][:, :], qh[:, r], ALU.mult).then_inc(dve_took, 1)
                if HGATE <= e < HGATE + 2:
                    r = e - HGATE
                    dve.wait_ge(sig_done, r + 3)
                    for t, src in enumerate((pw[s], pv[s])):
                        d = sgh[:, t, r * 256:(r + 1) * 256]
                        last = v.tensor_tensor(d, src[:, 0:256], d, ALU.mult)
                    last.then_inc(dve_took, 1)
                if b == 4:
                    dve.wait_ge(act_took, evac_count(HF + 1))
                    for c in range(HG):
                        q = slice(c * T, (c + 1) * T)
                        last = v.tensor_scalar(lf[:, q], lf[:, q], om_lb[:, c:c + 1], lb_col[:, c:c + 1], ALU.mult, ALU.add)
                    link(last)
                    v.tensor_scalar(kh[:, :], lf[:, :], -1.0, 1.0, ALU.mult, ALU.add).then_inc(f_ready, 1)
                if b == 10:
                    dve.wait_ge(lf_ready, 1)
                    dve.wait_ge(consts, 5)
                    link(v.tensor_tensor_scan(bcum[:, :], scan_m[:, :], lf[:, :], 0.0, ALU.mult, ALU.add))
                    bc = bcum[:, :].rearrange("p (n c) -> p n c", c=CH)
                    full = [P, HG * NCH, CH]
                    v.tensor_tensor(q_e[:, :].rearrange("p (n c) -> p n c", c=CH), bc,
                                    bc[:, :, CH // 2:CH // 2 + 1].broadcast_to(full), ALU.subtract).then_inc(d_ready, 1)
                    v.tensor_tensor(k_l[:, :].rearrange("p (n c) -> p n c", c=CH),
                                    bc[:, :, CH - 1:CH].broadcast_to(full), bc, ALU.subtract).then_inc(d_ready, 1)
                if b == 12:
                    dve.wait_ge(e_ready, 1)
                    v.tensor_tensor(k_e[:, :], k_e[:, :], kh[:, :], ALU.mult)
                    v.tensor_tensor(q_e[:, :], q_e[:, :], qh[:, :], ALU.mult).then_inc(qk_ready, 1)
                if b == 13:
                    v.tensor_tensor(k_l[:, :], k_l[:, :], kh[:, :], ALU.mult)
                    v.tensor_tensor(q_x[:, :], q_x[:, :], qh[:, :], ALU.mult).then_inc(qk_ready, 1)
                for n in range(NCH - 1):
                    if b == (18, 19, 19)[n]:
                        dve.wait_ge(ds_done, n + 1)
                        src = (pv[0], pv[1], px[3])[n]
                        if n == 0:
                            mark(v.tensor_copy(state[:, 0], src[:, :]), state_ready, 1)
                        else:
                            dec = decay[:, :].rearrange("p (h n) -> p h n", n=NCH)[:, :, n:n + 1].broadcast_to([P, HG, P])
                            link(v.tensor_tensor(state[:, n].rearrange("p (h d) -> p h d", h=HG),
                                                 state[:, n - 1].rearrange("p (h d) -> p h d", h=HG), dec, ALU.mult))
                            mark(v.tensor_tensor(state[:, n], state[:, n], src[:, :], ALU.add), state_ready, n + 1)
                if b == 21:
                    sq = qh[:, :].rearrange("p (a n) -> p a n", a=TT)
                    for t in range(TT):
                        dve.wait_ge(o_copied, t + 1)
                        last = v.tensor_tensor(sq[:, t], o_nat[:, t], o_nat[:, t], ALU.mult)
                    link(last)
                    link(v.tensor_reduce(sumsq[:, :], qh[:, :].rearrange("p (g d) -> p g d", d=P), AX, ALU.add))
                    v.tensor_scalar(sumsq[:, :], sumsq[:, :], 1.0 / P, RMS_EPS, ALU.mult, ALU.add).then_inc(ss_ready, 1)
                h = b - 15
                if 0 <= h < HEADS:
                    x = h % 2
                    dve.wait_ge(p_exp, h + 1)
                    link(v.reciprocal(rinv[:, 2 * x:2 * x + 2], rsum[:, 2 * x:2 * x + 2]))
                    v.tensor_scalar(prob[:, x, 0:P], prob[:, x, 0:P], rinv[:, 2 * x:2 * x + 1], None, ALU.mult)
                    v.tensor_scalar(prob[:, x, P:3 * P], prob[:, x, P:3 * P], rinv[:, 2 * x + 1:2 * x + 2], None,
                                    ALU.mult).then_inc(p_ready, 1)
                if b == 21:
                    dve.wait_ge(rms_ready, 1)
                    link(v.reciprocal(rms_i[:, :], rms[:, :]))
                    dve.wait_ge(norm_landed, 16)
                    ov = o_nat[:, :, :].rearrange("p a (h d) -> p (a h) d", d=P)
                    link(v.tensor_tensor(ov, ov, rms_i[:, :].unsqueeze(2).broadcast_to([P, TT * HG, P]), ALU.mult))
                    link(v.tensor_tensor(o_nat[:, :, :], o_nat[:, :, :], norm_g[:, :].unsqueeze(1).broadcast_to([P, TT, HG * P]), ALU.mult))
                    v.tensor_tensor(o_nat[:, :, :], o_nat[:, :, :], sgh[:, :, :], ALU.mult).then_inc(yb_ready, 1)
                for t in ada_at(b):
                    sum_ada(t)
                if b == 23:
                    dve.wait_ge(act_hi, 3)
                    v.tensor_tensor(a_lo[:, 0:4], yaT[:, :, :], a_hi[:, 0:4].bitcast(F32), ALU.subtract).then_inc(act_lo, 1)
                    dve.wait_ge(act_hi, 4)
                    for t, src in enumerate((pv[1], px[3])):
                        q = slice(t * P, (t + 1) * P)
                        last = v.tensor_tensor(a_lo[:, 4:8, q], src[:, :].rearrange("p (h t) -> p h t", h=HG),
                                               a_hi[:, 4:8, q].bitcast(F32), ALU.subtract)
                    last.then_inc(act_lo, 1)
                if BRANCH <= e < BRANCH + 4:
                    r = e - BRANCH
                    q = slice(2 * r, 2 * r + 2)
                    dve.wait_ge(gates_ready, 1)
                    dve.wait_ge(piece_used, 2 * e + 2)
                    if r >= 1:
                        dve.wait_ge(m_hi_ready, r)
                    v.tensor_tensor(br_a[:, :], pw[s][:, :], sig_a[:, q].rearrange("p c t -> p (c t)"), ALU.mult)
                    ins = v.tensor_tensor(br_b[:, :], pv[s][:, :], sig_b[:, q].rearrange("p c t -> p (c t)"), ALU.mult)
                    mark(ins, dve_took, evac_count(e))
                    mark(v.tensor_tensor(mix[:, :], br_a[:, :], br_b[:, :], ALU.add), mix_ready, r + 1)
                    split_lo_piece(b, b, 1)
                    dve.wait_ge(m_hi_ready, r + 1)
                    mark(v.tensor_tensor(m_lo[:, q].rearrange("p c t -> p (c t)"), mix[:, :],
                                         m_hi[:, q].rearrange("p c t -> p (c t)").bitcast(F32), ALU.subtract), m_lo_ready, r + 1)
                if b == WOUT + 1:
                    dve.wait_ge(gt1_done, 1)
                    v.tensor_copy(gt1[:, 0:512], px[0][:, :])
                    mark(v.tensor_copy(gt1[:, 512:1024], px[1][:, :]), gt1_ready, 1)
                if WOUT <= e < WQ:
                    r = e - WOUT
                    q = slice(r * 256, (r + 1) * 256)
                    dve.wait_ge(piece_used, 2 * e + 2)
                    if r == 0:
                        dve.wait_ge(x_landed, 64)
                    for t, src in enumerate((pw[s], pv[s])):
                        last = v.tensor_tensor(x1[:, t, q], src[:, 0:256], gt1[:, q], ALU.mult)
                    mark(last, dve_took, evac_count(e))
                    for t in range(TT):
                        last = v.scalar_tensor_tensor(x1[:, t, q], x_nat[:, t, q], ALPHA, x1[:, t, q], ALU.mult, ALU.add)
                    link(last)
                    for t in range(TT):
                        last = v.bn_stats(bn[:, (4 * t + r) * 6:(4 * t + r + 1) * 6], x1[:, t, q])
                    if r == 1:
                        dve.wait_ge(mod2_done, 1)
                        v.tensor_copy(mod2[:, 0:KC], px[2][:, 0:KC])
                        link(v.tensor_scalar(mod2[:, KC:2 * KC], px[2][:, KC:2 * KC], 1.0, None, ALU.add))
                        link(v.tensor_tensor(sb_cols[:, :], ln_cols[:, 0:KC], mod2[:, KC:2 * KC], ALU.mult))
                        v.tensor_tensor(mod2[:, 0:KC], mod2[:, 0:KC], sb_cols[:, :], ALU.add)
                        v.tensor_tensor(mod2[:, KC:2 * KC], mod2[:, KC:2 * KC], ln_cols[:, KC:2 * KC], ALU.mult).then_inc(mod2_ln_ready, 1)
                    if r == 2:
                        dve.wait_ge(gt2_done, 1)
                        for half in range(2):
                            ins = v.tensor_copy(gt2_row[0:1, half * 512:(half + 1) * 512], px[half][0:1, :])
                        ins.then_inc(gt2_ready, 1)
                    if r == 3:
                        link(last)
                        for t in range(TT):
                            last = v.bn_aggr(mv[:, 2 * t:2 * t + 2], bn[:, 24 * t:24 * t + 24])
                        link(last)
                        v.tensor_scalar(std[:, :], mv[:, :].rearrange("p (t x) -> p t x", x=2)[:, :, 1], LN_EPS, None,
                                        ALU.add).then_inc(var_ready, 1)
                        dve.wait_ge(std_ready, 1)
                        link(v.reciprocal(rstd[:, :], std[:, :]))
                        for t in range(TT):
                            v.tensor_scalar(x1[:, t], x1[:, t], mv[:, 2 * t:2 * t + 1], rstd[:, t:t + 1], ALU.subtract, ALU.mult) \
                                .then_inc(xn_ready, 1)
                        dve.wait_ge(mod2_ln_ready, 1)
                        dve.wait_ge(x1T_done, 1)
                        for k in range(KC // 2):
                            ins = v.tensor_scalar(h2f[:, k], px[k // 2][:, (k % 2) * T:(k % 2 + 1) * T],
                                                  mod2[:, KC + k:KC + k + 1], mod2[:, k:k + 1], ALU.mult, ALU.add)
                        mark(ins, h2f_ready, 1)
                        act_split_lo(h2f, 4)
                if b >= NA - TT:
                    t = b - (NA - TT)
                    link(v.tensor_tensor(x1[:, t], x1[:, t], ln1_g[:, :], ALU.mult))
                    v.tensor_tensor(x1[:, t], x1[:, t], ln1_b[:, :], ALU.add).then_inc(x1_ready, 1)

            split_lo(U0, U0)
            iota16 = iota[:, 0:TOPK]

            def go(ins):
                chain["n"] += 1
                ins.then_inc(dve_chain, 1)
                return chain["n"]

            def need(c, alone=False):
                dve.wait_ge(dve_chain, chain["at"] + c)
                if alone:
                    v.nop(nofuse=True)

            start, per_unit = chain["n"], 22
            with dve.Fori(0, G1 // 2) as i:
                chain["at"], chain["n"] = per_unit * i + start, 0
                dve.wait_ge(s_in_ready, i + 1)
                v.nop(nofuse=True)
                first = [go(v.max(top_v[:, a, 0:8], s_in[:, a])) for a in range(2)]
                cut = []
                for a in range(2):
                    need(first[a], alone=True)
                    v.max_index(top_i[:, a, 0:8], top_v[:, a, 0:8], s_in[:, a])
                    cut.append(go(v.match_replace(s_cut[:, a], top_v[:, a, 0:8], s_in[:, a], NEG)))
                second = []
                for a in range(2):
                    need(cut[a], alone=True)
                    second.append(go(v.max(top_v[:, a, 8:16], s_cut[:, a])))
                for a in range(2):
                    need(second[a], alone=True)
                    found = go(v.max_index(top_i[:, a, 8:16], top_v[:, a, 8:16], s_cut[:, a]))
                made = go(v.tensor_tensor(cand[:, :, :], top_v[:, 0].unsqueeze(2).broadcast_to([P, TOPK, TOPK]),
                                          top_v[:, 1].unsqueeze(1).broadcast_to([P, TOPK, TOPK]), ALU.add))
                need(found)
                named = go(v.tensor_copy(top_f[:, :, :], top_i[:, :, :]))
                flat = cand[:, :, :].rearrange("p a b -> p (a b)")
                need(made, alone=True)
                first = go(v.max(best_t[:, 0:8], flat))
                need(first, alone=True)
                v.max_index(pos[:, 0:8], best_t[:, 0:8], flat)
                cut = go(v.match_replace(c_cut[:, :], best_t[:, 0:8], flat, NEG))
                need(cut, alone=True)
                second = go(v.max(best_t[:, 8:16], c_cut[:, :]))
                need(second, alone=True)
                found = go(v.max_index(pos[:, 8:16], best_t[:, 8:16], c_cut[:, :]))
                v.tensor_copy(best[:, bass.ds(i, 1)].rearrange("p a k -> p (a k)"), best_t[:, :])
                need(found)
                v.tensor_single_scalar(pos2[:, 0], pos[:, :], 4, op=ALU.logical_shift_right)
                halves = go(v.tensor_single_scalar(pos2[:, 1], pos[:, :], TOPK - 1, op=ALU.bitwise_and))
                need(halves)
                places = go(v.tensor_copy(posf[:, :, :], pos2[:, :, :]))
                need(places)
                hit = [go(v.tensor_tensor(eq[:, a], posf[:, a].unsqueeze(2).broadcast_to([P, TOPK, TOPK]),
                                          iota16.unsqueeze(1).broadcast_to([P, TOPK, TOPK]), ALU.is_equal)) for a in range(2)]
                need(named)
                key = []
                for a in range(2):
                    need(hit[a])
                    key.append(go(v.tensor_tensor(eq[:, a], eq[:, a], top_f[:, a].unsqueeze(1).broadcast_to([P, TOPK, TOPK]),
                                                  ALU.mult)))
                for a in range(2):
                    need(key[a])
                    last = go(v.tensor_reduce(ij[:, a, bass.ds(i, 1)].rearrange("p a k -> p (a k)"), eq[:, a], AX, ALU.add))
                need(last)
                v.tensor_copy(best_t[:, 0:1], best_t[:, 0:1]).then_inc(s_in_used, 1)
                assert chain["n"] == per_unit, chain["n"]
            chain["at"], chain["n"] = None, start + per_unit * (G1 // 2)
            link(v.tensor_tensor(gate[:, :, :], best[:, :, :], best[:, :, 0:1].broadcast_to([P, TT * PH, TOPK]), ALU.subtract))
            mark(v.tensor_copy(mv[:, 0:1], mv[:, 0:1]), best_ready, 1)
            dve.wait_ge(gate_exp, 1)
            link(v.tensor_reduce(gsum[:, :], gate[:, :, :], AX, ALU.add))
            link(v.reciprocal(ginv[:, :], gsum[:, :]))
            v.tensor_tensor(gate[:, :, :], gate[:, :, :], ginv[:, :].unsqueeze(2).broadcast_to([P, TT * PH, TOPK]),
                            ALU.mult).then_inc(gate_ready, 1)
            for t in range(TT):
                dve.wait_ge(idxT_done, 2)
                v.tensor_copy(idx[:, 2, t * P:(t + 1) * P], px[3][:, t * P:(t + 1) * P]).then_inc(g_lo_taken, S_OH // 2)
            dve.wait_ge(g_hi_taken, S_OH)
            dve.wait_ge(g_lo_taken, S_OH)

            def one_hot_i(i, e):
                dve.wait_ge(oh_used, S_OH * i + (e + 1))
                for y in range(4):
                    t = 4 * S_OH * i + (4 * e + y)
                    last = v.tensor_scalar(oh_i[e % S_OH][:, y], iota[:, :], idx[:, 0, bass.ds(t, 1)],
                                           idx[:, 2, bass.ds(t, 1)], ALU.is_equal, ALU.mult)
                last.then_inc(ohi_ready, 1)

            def take_lower(i, e):
                dve.wait_ge(g_hi_taken, S_OH * i + (S_OH + e + 1))
                w = W[:, 0:2 * G1, bass.ds(4 * S_OH * i + 4 * e, 4)]
                v.tensor_tensor(w, pg[e][:, :].rearrange("p (t j) -> p j t", t=4)[:, 0:2 * G1], w, ALU.mult) \
                    .then_inc(g_lo_taken, 1)

            for e in range(2):
                one_hot_i(0, e)
            with dve.Fori(0, GROUPS // S_OH - 1) as i:
                for e in range(S_OH):
                    one_hot_i(i, e + 2)
                    take_lower(i, e)
            for e in range(S_OH):
                if e + 2 < S_OH:
                    one_hot_i(GROUPS // S_OH - 1, e + 2)
                take_lower(GROUPS // S_OH - 1, e)

            def product(q):
                dve.wait_ge(u_taken, q + (G1 + 3))
                w = W[:, bass.ds(2 * q + 2 * G1, 2)].rearrange("p a t -> p (a t)")
                v.tensor_tensor(w, w, gel[:, :], ALU.mult).then_inc(prod_ready, 1)

            def w_lo_part(pair, split, e):
                dve.wait_ge(wsplit_hi, split + (e + 1))
                v.tensor_tensor(ws_lo[:, e], W[:, bass.ds(2 * pair + e, 1)].rearrange("p a t -> p (a t)"),
                                ws_hi[:, e].bitcast(F32), ALU.subtract).then_inc(wsplit_lo, 1)

            dve.wait_ge(g_hi_taken, GROUPS + S_OH)
            dve.wait_ge(lo_ready, 2 * (U0 + G1) + 2)
            product(0)
            with dve.Fori(0, STEPS) as q:
                split_lo(2 * q + U2, U2)
                for e in range(2):
                    w_lo_part(q + G1, 2 * q, e)
                split_lo(2 * q + (U2 + 1), U2 + 1)
                product(q + 1)
            split_lo(V2, V2)
            for e in range(2):
                w_lo_part(NG - 1, 2 * STEPS, e)
            with dve.Fori(0, G1 // 2) as i:
                for x in range(2):
                    n0 = V2 + 1 + x
                    split_lo(2 * i + n0, n0)
                    for e in range(2):
                        w_lo_part(2 * i + x, 4 * i + 2 * (STEPS + 1 + x), e)
            dve.wait_ge(end_landed, 64)

            def residual(t):
                dve.wait_ge(y_done, t + 1)
                for half in range(2):
                    q = slice(half * 512, (half + 1) * 512)
                    last = v.tensor_tensor(z2[:, t, q], px[2 * t + half][:, :], gt2_b[:, q], ALU.mult)
                link(last)
                link(v.scalar_tensor_tensor(z2[:, t], x1_b[:, t], ALPHA, z2[:, t], ALU.mult, ALU.add))

            def statistics(t):
                for half in range(2):
                    i = (2 * t + half) * 6
                    last = v.bn_stats(bn[:, i:i + 6], z2[:, t, half * 512:(half + 1) * 512])
                link(last)
                link(v.bn_aggr(mv[:, 2 * t:2 * t + 2], bn[:, 12 * t:12 * t + 12]))
                v.tensor_scalar(std[:, t:t + 1], mv[:, 2 * t + 1:2 * t + 2], LN_EPS, None, ALU.add).then_inc(var2_ready, 1)

            def normalise(t):
                dve.wait_ge(std2_ready, t + 1)
                link(v.reciprocal(rstd[:, t:t + 1], std[:, t:t + 1]))
                return v.tensor_scalar(z2[:, t], z2[:, t], mv[:, 2 * t:2 * t + 1], rstd[:, t:t + 1], ALU.subtract, ALU.mult)

            residual(0)
            statistics(0)
            normalise(0).then_inc(zn_ready, 1)
            residual(1)
            statistics(1)
            link(normalise(1))
            link(v.tensor_tensor(z2[:, 1], z2[:, 1], ln2_g[:, :], ALU.mult))
            v.tensor_tensor(z2[:, 1], z2[:, 1], ln2_b[:, :], ALU.add).then_inc(z2_ready[1], 1)


def kernel(**inputs):
    import numpy as np
    import concourse.bacc as bacc
    from concourse.bass_utils import run_bass_kernel_spmd

    a = {k: np.asarray(x) for k, x in inputs.items()}

    def columns(w):
        n = w.shape[1] // 256
        return w.reshape(KC, P, n, 2, P).transpose(2, 1, 3, 0, 4).reshape(n, P, 2048)

    def rows(w):
        n = w.shape[1] // 256
        return w.reshape(KC, P, n, 256).transpose(2, 1, 0, 3).reshape(n, P, 2048)

    w_in = a["w_in"][0]
    cuts = np.cumsum([512] * 7 + [1024])
    qa, ka, va, hq, hf, hi, hg, ga, gb = np.split(w_in, cuts, axis=1)
    br = [a[k][0].reshape(HG, P, 4, 256).transpose(2, 1, 0, 3).reshape(4, P, 1, 1024) for k in ("w_branch_a", "w_branch_b")]
    ws = np.concatenate([columns(hf), columns(hq), rows(hi), rows(hg), columns(qa), columns(ka), rows(va),
                         columns(ga), columns(gb), np.concatenate(br, axis=2).reshape(4, P, 2048),
                         rows(a["w_out"][0]), columns(a["peer_wq"][0])])
    u = a["peer_u"][0].reshape(P, NG, 2, KC, P).transpose(1, 4, 2, 3, 0).reshape(NG, P, 2048)
    v = a["peer_v"][0].reshape(P, NG, 2 * D).transpose(1, 0, 2)
    arrays = {
        "xT": a["x"][0].T, "x": a["x"][0], "c": a["c"][0].reshape(KC, P).T, "w_ada": a["w_ada"][0], "b_ada": a["b_ada"],
        "ws": ws, "lb": a["hgrn_lb"].reshape(2, HG, P).transpose(2, 0, 1).reshape(P, 2 * HG),
        "norm_g": a["hgrn_norm_g"][0], "ln1_g": a["ln1_g"][0], "ln1_b": a["ln1_b"][0],
        "ln1_cols": np.concatenate([a[k][0].reshape(KC, P).T for k in ("ln1_b", "ln1_g")], axis=1),
        "keys": a["peer_subkeys"][0].transpose(1, 3, 0, 2).reshape(P, PH, NK),
        "u": u, "v": v, "ln2_g": a["ln2_g"][0], "ln2_b": a["ln2_b"][0],
    }
    arrays = {"in_" + k: np.ascontiguousarray(x) for k, x in arrays.items()}
    nc = bacc.Bacc("TRN2", target_bir_lowering=False, num_devices=1)
    args = [nc.dram_tensor(k, x.shape, mybir.dt.from_np(x.dtype), kind="ExternalInput").ap() for k, x in arrays.items()]
    args.append(nc.dram_tensor("x1_spill", (T, D), F32).ap())
    args.append(nc.dram_tensor("gate2_spill", (1, D), F32).ap())
    args.append(nc.dram_tensor("out_0", (T, D), F32, kind="ExternalOutput").ap())
    layer(nc, *args)
    r = run_bass_kernel_spmd(nc, [arrays], core_ids=[0])
    return r.results[0]["out_0"].reshape(1, T, D)
```
